# Optimizing a Trainium2 kernel written in Bass

```python
import jax, jax.numpy as jnp
from jax import lax
import numpy as np
import math
import jax
import jax.numpy as jnp

D_MODEL = 1024
BATCH = 1
SEQ = 1024
DEPTH = 1

HEAD_DIM = 64
SB_HEADS = 8
SB_WIDTH = SB_HEADS * HEAD_DIM
CONV_GROUPS = 4
CONV_WIDTH_CH = CONV_GROUPS * HEAD_DIM
MEM_HEADS = 4
MEM_WIDTH = MEM_HEADS * HEAD_DIM
MIX_WIDTH = SB_WIDTH + CONV_WIDTH_CH + MEM_WIDTH
N_MEM = 256
CONV_K = 3
SB_BLOCK = 128
EPS = 1e-6

SPLIT_POINTS = [
    SB_WIDTH,
    2 * SB_WIDTH,
    3 * SB_WIDTH,
    3 * SB_WIDTH + CONV_WIDTH_CH,
    3 * SB_WIDTH + 2 * CONV_WIDTH_CH,
    3 * SB_WIDTH + 3 * CONV_WIDTH_CH,
    3 * SB_WIDTH + 3 * CONV_WIDTH_CH + MEM_WIDTH,
]
PROJ_WIDTH = 3 * SB_WIDTH + 3 * CONV_WIDTH_CH + MEM_WIDTH + MIX_WIDTH


def _rmsnorm(x, g):
    xf = x.astype(jnp.float32)
    y = xf * lax.rsqrt(jnp.mean(xf * xf, axis=-1, keepdims=True) + EPS)
    return (y * g.astype(jnp.float32)).astype(x.dtype)

def _stick_breaking_attention(q, k, v):
    b, t, h, dh = q.shape
    nblk = t // SB_BLOCK
    scale = dh ** -0.5
    key_pos = jnp.arange(t)
    q_blocks = q.reshape(b, nblk, SB_BLOCK, h, dh).transpose(1, 0, 2, 3, 4)
    starts = jnp.arange(nblk) * SB_BLOCK

    def block(args):
        q_blk, start = args
        q_pos = start + jnp.arange(SB_BLOCK)
        z = jnp.einsum('bqhd,bkhd->bhqk', q_blk, k,
                       preferred_element_type=jnp.float32) * scale
        before = key_pos[None, :] < q_pos[:, None]
        log_not = jnp.where(before, jax.nn.log_sigmoid(-z), 0.0)
        suffix = lax.cumsum(log_not, axis=3, reverse=True) - log_not
        w = jnp.where(before, jnp.exp(jax.nn.log_sigmoid(z) + suffix), 0.0)
        return jnp.einsum('bhqk,bkhd->bqhd', w.astype(v.dtype), v)

    out = lax.map(block, (q_blocks, starts))
    return out.transpose(1, 0, 2, 3, 4).reshape(b, t, h, dh)

def _causal_depthwise_conv(u, w, bias):
    c = u.shape[-1]
    y = lax.conv_general_dilated(
        u, w[:, None, :].astype(u.dtype), window_strides=(1,),
        padding=[(CONV_K - 1, 0)], dimension_numbers=('NWC', 'WIO', 'NWC'),
        feature_group_count=c)
    return y + bias.astype(u.dtype)

def _memory_attention(q, mk, mv):
    s = jnp.einsum('bthd,bmhd->bhtm', q, mk,
                   preferred_element_type=jnp.float32) * (q.shape[-1] ** -0.5)
    p = jax.nn.softmax(s, axis=-1)
    return jnp.einsum('bhtm,bmhd->bthd', p.astype(mv.dtype), mv)

def first_inputs(seed: int = 0) -> dict:
    key = jax.random.key(seed)
    ks = jax.random.split(key, 14)
    f32 = jnp.float32
    x = jax.random.normal(ks[0], (BATCH, SEQ, D_MODEL), f32)
    mem = jax.random.normal(ks[1], (BATCH, N_MEM, D_MODEL), f32)
    g_in = 1.0 + 0.02 * jax.random.normal(ks[2], (DEPTH, D_MODEL), f32)
    w_in = jax.random.normal(ks[3], (DEPTH, D_MODEL, PROJ_WIDTH), f32) * D_MODEL ** -0.5
    conv_w = jax.random.normal(ks[4], (DEPTH, CONV_K, CONV_WIDTH_CH), f32) * CONV_K ** -0.5
    conv_b = 0.01 * jax.random.normal(ks[5], (DEPTH, CONV_WIDTH_CH), f32)
    g_mem = 1.0 + 0.02 * jax.random.normal(ks[6], (DEPTH, D_MODEL), f32)
    w_mem_kv = jax.random.normal(ks[7], (DEPTH, D_MODEL, 2 * MEM_WIDTH), f32) * D_MODEL ** -0.5
    g_sb_out = 1.0 + 0.02 * jax.random.normal(ks[8], (DEPTH, SB_WIDTH), f32)
    g_conv_out = 1.0 + 0.02 * jax.random.normal(ks[9], (DEPTH, CONV_WIDTH_CH), f32)
    g_mem_out = 1.0 + 0.02 * jax.random.normal(ks[10], (DEPTH, MEM_WIDTH), f32)
    w_out = jax.random.normal(ks[11], (DEPTH, MIX_WIDTH, D_MODEL), f32) * MIX_WIDTH ** -0.5
    g_final = 1.0 + 0.02 * jax.random.normal(ks[12], (D_MODEL,), f32)
    return {"x": x, "mem": mem, "g_in": g_in, "w_in": w_in, "conv_w": conv_w,
            "conv_b": conv_b, "g_mem": g_mem, "w_mem_kv": w_mem_kv,
            "g_sb_out": g_sb_out, "g_conv_out": g_conv_out, "g_mem_out": g_mem_out,
            "w_out": w_out, "g_final": g_final}

def first_block(x, mem, g_in, w_in, conv_w, conv_b, g_mem, w_mem_kv,
              g_sb_out, g_conv_out, g_mem_out, w_out, g_final):
    b, t, _ = x.shape
    for l in range(DEPTH):
        h = _rmsnorm(x, g_in[l])
        proj = h @ w_in[l]
        q_sb, k_sb, v_sb, u_c, b_c, c_c, q_mem, gate = jnp.split(proj, SPLIT_POINTS, axis=-1)

        y_sb = _stick_breaking_attention(
            q_sb.reshape(b, t, SB_HEADS, HEAD_DIM),
            k_sb.reshape(b, t, SB_HEADS, HEAD_DIM),
            v_sb.reshape(b, t, SB_HEADS, HEAD_DIM)).reshape(b, t, SB_WIDTH)

        y_conv = b_c * _causal_depthwise_conv(c_c * u_c, conv_w[l], conv_b[l])

        m = _rmsnorm(mem, g_mem[l])
        mk, mv = jnp.split(m @ w_mem_kv[l], 2, axis=-1)
        nm = mem.shape[1]
        y_mem = _memory_attention(
            q_mem.reshape(b, t, MEM_HEADS, HEAD_DIM),
            mk.reshape(b, nm, MEM_HEADS, HEAD_DIM),
            mv.reshape(b, nm, MEM_HEADS, HEAD_DIM)).reshape(b, t, MEM_WIDTH)

        y = jnp.concatenate([_rmsnorm(y_sb, g_sb_out[l]),
                             _rmsnorm(y_conv, g_conv_out[l]),
                             _rmsnorm(y_mem, g_mem_out[l])], axis=-1)
        x = x + (y * jax.nn.silu(gate)) @ w_out[l]
    return _rmsnorm(x, g_final)


_first_inputs = first_inputs


def first_inputs(seed=0):
    import zlib

    import numpy as np

    out = dict(_first_inputs(seed))
    spreads = {}
    factors = {'g_in': 3.234,
     'conv_b': 64.0,
     'g_mem': 6.955,
     'g_sb_out': 33.684,
     'g_conv_out': 48.437,
     'g_mem_out': 44.203,
     'g_final': 8.356}
    for name, (base, spread) in spreads.items():
        noise = np.random.default_rng([zlib.crc32(name.encode()), seed]).standard_normal(out[name].shape)
        drawn = base * np.exp(spread * noise) if base else spread * noise
        out[name] = __import__('jax').numpy.asarray(drawn.astype(out[name].dtype))
    for name, factor in factors.items():
        out[name] = (out[name] * factor).astype(out[name].dtype)
    return out


_narrow_inputs = first_inputs


def first_inputs(seed=0):

    out = dict(_narrow_inputs(seed))
    wider = {'g_sb_out': 5.62, 'g_conv_out': 5.8, 'g_mem_out': 5.67, 'g_final': 3.26}
    for name, times in wider.items():
        mean = out[name].mean()
        out[name] = (mean + times * (out[name] - mean)).astype(out[name].dtype)
    return out


GRID_W = 64
CTX_LEN = 256

N_Q_HEADS = 8
N_KV_HEADS = 2
Q_GROUP = N_Q_HEADS // N_KV_HEADS
ATT_Q_W = N_Q_HEADS * HEAD_DIM
ATT_KV_W = N_KV_HEADS * HEAD_DIM
Q_BLOCK = 128
ROPE_THETA = 10000.0
ROPE_AXIS_DIM = HEAD_DIM // 2

HY_W = D_MODEL // 4
HY_ORDER = 2
HY_SHORT = 3
HY_BANDS = 16
HY_EMB = 2 * HY_BANDS + 1
HY_FFN = 64
HY_DECAY_TARGET = 1e-2
HY_DECAY_SHORT_PCT = 0.3
HY_DECAY_LONG_PCT = 1.5

FN_GROUPS = 4
FN_GROUP_W = D_MODEL // 16
FN_W = FN_GROUPS * FN_GROUP_W

MIX_W = ATT_Q_W + HY_W + FN_W
N_BRANCH = 3

OFF_Q = 0
OFF_K = OFF_Q + ATT_Q_W
OFF_V = OFF_K + ATT_KV_W
OFF_HY = OFF_V + ATT_KV_W
OFF_FN = OFF_HY + (HY_ORDER + 1) * HY_W
OFF_GATE = OFF_FN + FN_W
IN_W = OFF_GATE + N_BRANCH * D_MODEL

N_EXPERTS = 16
EXPERT_FF = 2 * D_MODEL
CAPACITY_FACTOR = 2


def rms_norm(x, g):
    xf = x.astype(jnp.float32)
    y = xf * lax.rsqrt(jnp.mean(xf * xf, axis=-1, keepdims=True) + EPS)
    return (y * g.astype(jnp.float32)).astype(x.dtype)

def modulate(h, shift, scale):
    return h * (1.0 + scale) + shift

def axial_rope_tables(n_tokens):
    rows = n_tokens // GRID_W
    row = jnp.repeat(jnp.arange(rows, dtype=jnp.float32), GRID_W)
    col = jnp.tile(jnp.arange(GRID_W, dtype=jnp.float32), rows)
    inv = ROPE_THETA ** (-jnp.arange(0, ROPE_AXIS_DIM, 2, dtype=jnp.float32) / ROPE_AXIS_DIM)
    ang = jnp.concatenate([row[:, None] * inv, col[:, None] * inv], axis=-1)
    return jnp.cos(ang), jnp.sin(ang)

def apply_rope(u, cos, sin):
    uf = u.astype(jnp.float32).reshape(*u.shape[:-1], HEAD_DIM // 2, 2)
    u0, u1 = uf[..., 0], uf[..., 1]
    c = cos[None, :, None, :]
    s = sin[None, :, None, :]
    out = jnp.stack([u0 * c - u1 * s, u0 * s + u1 * c], axis=-1)
    return out.reshape(u.shape).astype(u.dtype)

def qk_heads(u, n_heads, gain, rope):
    b, n, _ = u.shape
    u = rms_norm(u.reshape(b, n, n_heads, HEAD_DIM), gain)
    if rope is not None:
        u = apply_rope(u, rope[0], rope[1])
    return u

def block_attention(q, k, v):
    b, n = q.shape[0], q.shape[1]
    nb = n // Q_BLOCK
    qb = q.reshape(b, nb, Q_BLOCK, N_KV_HEADS, Q_GROUP, HEAD_DIM).transpose(1, 0, 2, 3, 4, 5)
    scale = HEAD_DIM ** -0.5

    def attend(qblk):
        s = jnp.einsum('bqkgd,bskd->bkgqs', qblk, k, preferred_element_type=jnp.float32) * scale
        p = jax.nn.softmax(s, axis=-1).astype(v.dtype)
        return jnp.einsum('bkgqs,bskd->bqkgd', p, v)

    o = lax.map(attend, qb)
    return o.transpose(1, 0, 2, 3, 4, 5).reshape(b, n, ATT_Q_W)

def short_conv(u, w, b):
    n = u.shape[1]
    pad = HY_SHORT // 2
    up = jnp.pad(u, ((0, 0), (pad, pad), (0, 0)))
    out = b
    for j in range(HY_SHORT):
        out = out + up[:, j:j + n] * w[j]
    return out

def hyena_spectrum(n, w1, b1, w2, b2, w3, freq):
    f32 = jnp.float32
    w1, b1, w2, b2, w3, freq = (a.astype(f32) for a in (w1, b1, w2, b2, w3, freq))
    pos = jnp.arange(n, dtype=f32)
    t = pos / (n - 1)
    bands = jnp.linspace(1e-4, HY_BANDS - 1, HY_BANDS, dtype=f32)
    ang = (2.0 * math.pi / n) * pos[:, None] * bands[None, :]
    feats = jnp.concatenate([t[:, None], jnp.cos(ang), -jnp.sin(ang)], axis=-1)
    h = jnp.sin(freq * (feats @ w1 + b1))
    h = jnp.sin(freq * (h @ w2 + b2))
    h = (h @ w3).reshape(n, 2, HY_ORDER, HY_W)
    deltas = jnp.abs(jnp.linspace(math.log(HY_DECAY_TARGET) / HY_DECAY_LONG_PCT,
                                  math.log(HY_DECAY_TARGET) / HY_DECAY_SHORT_PCT, HY_W, dtype=f32))
    h = h * jnp.exp(-t[:, None] * deltas[None, :])[:, None, None, :]
    filt = jnp.concatenate([h[:, 0], jnp.zeros((1, HY_ORDER, HY_W), f32), h[1:, 1][::-1]], axis=0)
    filt = filt / jnp.sum(jnp.abs(filt), axis=0, keepdims=True)
    return jnp.fft.rfft(filt, axis=0)

def long_conv(z, spec, d):
    n = z.shape[1]
    zf = z.astype(jnp.float32)
    y = jnp.fft.irfft(jnp.fft.rfft(zf, n=2 * n, axis=1) * spec[None], n=2 * n, axis=1)[:, :n]
    return (y + zf * d.astype(jnp.float32)).astype(z.dtype)

def hyena_mixer(u, sw, sb, spec, bias):
    u = short_conv(u, sw, sb)
    v, g1, g2 = jnp.split(u, HY_ORDER + 1, axis=-1)
    z = g1 * long_conv(v, spec[:, 0], bias[0])
    return g2 * long_conv(z, spec[:, 1], bias[1])

def fourier_mix(u):
    b, n, _ = u.shape
    ug = u.astype(jnp.float32).reshape(b, n, FN_GROUPS, FN_GROUP_W)
    y = jnp.fft.fft2(ug, axes=(1, 3), norm='ortho').real
    return y.reshape(b, n, FN_W).astype(u.dtype)

def merge_branches(att, hy, fn, gates, w_branch, w_out):
    ga, gh, gf = jnp.split(gates, N_BRANCH, axis=-1)
    ya = att @ w_branch[:ATT_Q_W]
    yh = hy @ w_branch[ATT_Q_W:ATT_Q_W + HY_W]
    yf = fn @ w_branch[ATT_Q_W + HY_W:]
    m = jax.nn.sigmoid(ga) * ya + jax.nn.sigmoid(gh) * yh + jax.nn.sigmoid(gf) * yf
    return m @ w_out

def mixer_sublayer(h, k_ext, v_ext, rope, w_in, q_gain, k_gain, sw, sb, spec, hy_bias, w_branch, w_out):
    b, n, _ = h.shape
    p = h @ w_in
    q = qk_heads(p[..., OFF_Q:OFF_K], N_Q_HEADS, q_gain, rope)
    k = qk_heads(p[..., OFF_K:OFF_V], N_KV_HEADS, k_gain, rope)
    v = p[..., OFF_V:OFF_HY].reshape(b, n, N_KV_HEADS, HEAD_DIM)
    if k_ext is None:
        att = block_attention(q, k, v)
    else:
        att = block_attention(q, jnp.concatenate([k, k_ext], axis=1), jnp.concatenate([v, v_ext], axis=1))
    hy = hyena_mixer(p[..., OFF_HY:OFF_FN], sw, sb, spec, hy_bias)
    fn = fourier_mix(p[..., OFF_FN:OFF_GATE])
    return merge_branches(att, hy, fn, p[..., OFF_GATE:], w_branch, w_out), k, v

def expert_choice_moe(h, w_router, w_gate, w_up, w_down):
    b, n, d = h.shape
    cap = CAPACITY_FACTOR * n // N_EXPERTS
    logits = jnp.einsum('bld,de->ble', h, w_router, preferred_element_type=jnp.float32)
    aff = jax.nn.softmax(logits, axis=-1)
    top_w, top_i = lax.top_k(aff.transpose(0, 2, 1), cap)
    xg = jax.vmap(lambda hb, ib: hb[ib])(h, top_i)
    a = jnp.einsum('becd,edf->becf', xg, w_gate)
    u = jnp.einsum('becd,edf->becf', xg, w_up)
    y = jnp.einsum('becf,efd->becd', jax.nn.silu(a) * u, w_down)
    y = y * top_w[..., None].astype(y.dtype)
    return jax.vmap(lambda yb, ib: jnp.zeros((n, d), y.dtype).at[ib.reshape(-1)].add(yb.reshape(-1, d)))(y, top_i)

def second_inputs(seed: int = 0) -> dict:
    key = jax.random.key(seed)
    ks = jax.random.split(key, 27)
    f32 = jnp.float32
    D = D_MODEL

    def nrm(k, shape, scale):
        return jax.random.normal(k, shape, f32) * scale

    return {
        "x": nrm(ks[0], (BATCH, SEQ, D), 1.0),
        "c": nrm(ks[1], (BATCH, D), 1.0),
        "ctx": nrm(ks[2], (BATCH, CTX_LEN, D), 1.0),
        "c_ctx": nrm(ks[3], (D,), 1.0),
        "w_mod": nrm(ks[4], (DEPTH, D, 6 * D), 0.5 * D ** -0.5),
        "b_mod": nrm(ks[5], (DEPTH, 6 * D), 0.02),
        "norm1_g": 1.0 + nrm(ks[6], (DEPTH, D), 0.02),
        "norm2_g": 1.0 + nrm(ks[7], (DEPTH, D), 0.02),
        "w_in": nrm(ks[8], (DEPTH, D, IN_W), D ** -0.5),
        "q_gain": 1.0 + nrm(ks[9], (DEPTH, HEAD_DIM), 0.02),
        "k_gain": 1.0 + nrm(ks[10], (DEPTH, HEAD_DIM), 0.02),
        "hy_short_w": nrm(ks[11], (DEPTH, HY_SHORT, (HY_ORDER + 1) * HY_W), HY_SHORT ** -0.5),
        "hy_short_b": nrm(ks[12], (DEPTH, (HY_ORDER + 1) * HY_W), 0.02),
        "hy_f_w1": nrm(ks[13], (DEPTH, HY_EMB, HY_FFN), HY_EMB ** -0.5),
        "hy_f_b1": nrm(ks[14], (DEPTH, HY_FFN), 0.1),
        "hy_f_w2": nrm(ks[15], (DEPTH, HY_FFN, HY_FFN), HY_FFN ** -0.5),
        "hy_f_b2": nrm(ks[16], (DEPTH, HY_FFN), 0.1),
        "hy_f_w3": nrm(ks[17], (DEPTH, HY_FFN, 2 * HY_ORDER * HY_W), HY_FFN ** -0.5),
        "hy_f_freq": 1.0 + nrm(ks[18], (DEPTH, HY_FFN), 0.02),
        "hy_bias": nrm(ks[19], (DEPTH, HY_ORDER, HY_W), 1.0),
        "w_branch": nrm(ks[20], (DEPTH, MIX_W, D), (MIX_W // 4) ** -0.5),
        "w_out": nrm(ks[21], (DEPTH, D, D), D ** -0.5),
        "w_router": nrm(ks[22], (DEPTH, D, N_EXPERTS), D ** -0.5),
        "w_gate": nrm(ks[23], (DEPTH, N_EXPERTS, D, EXPERT_FF), D ** -0.5),
        "w_up": nrm(ks[24], (DEPTH, N_EXPERTS, D, EXPERT_FF), D ** -0.5),
        "w_down": nrm(ks[25], (DEPTH, N_EXPERTS, EXPERT_FF, D), EXPERT_FF ** -0.5),
        "final_g": 1.0 + nrm(ks[26], (D,), 0.02),
    }

def second_block(x, c, ctx, c_ctx, w_mod, b_mod, norm1_g, norm2_g, w_in, q_gain, k_gain,
              hy_short_w, hy_short_b, hy_f_w1, hy_f_b1, hy_f_w2, hy_f_b2, hy_f_w3, hy_f_freq,
              hy_bias, w_branch, w_out, w_router, w_gate, w_up, w_down, final_g):
    n_lat = x.shape[1]
    n_ctx = ctx.shape[1]
    rope = axial_rope_tables(n_lat)
    sc = jax.nn.silu(c)
    scc = jax.nn.silu(c_ctx)
    for l in range(DEPTH):
        last = l == DEPTH - 1
        mx = (sc @ w_mod[l] + b_mod[l])[:, None, :]
        mc = scc @ w_mod[l] + b_mod[l]
        sh1, sc1, g1, sh2, sc2, g2 = jnp.split(mx, 6, axis=-1)
        csh1, csc1, cg1, csh2, csc2, cg2 = jnp.split(mc, 6, axis=-1)

        hc = modulate(rms_norm(ctx, norm1_g[l]), csh1, csc1)
        if last:
            pkv = hc @ w_in[l][:, OFF_K:OFF_HY]
            kc = qk_heads(pkv[..., :ATT_KV_W], N_KV_HEADS, k_gain[l], None)
            vc = pkv[..., ATT_KV_W:].reshape(ctx.shape[0], n_ctx, N_KV_HEADS, HEAD_DIM)
        else:
            spec_c = hyena_spectrum(n_ctx, hy_f_w1[l], hy_f_b1[l], hy_f_w2[l], hy_f_b2[l], hy_f_w3[l], hy_f_freq[l])
            yc, kc, vc = mixer_sublayer(hc, None, None, None, w_in[l], q_gain[l], k_gain[l],
                                        hy_short_w[l], hy_short_b[l], spec_c, hy_bias[l], w_branch[l], w_out[l])

        spec_x = hyena_spectrum(n_lat, hy_f_w1[l], hy_f_b1[l], hy_f_w2[l], hy_f_b2[l], hy_f_w3[l], hy_f_freq[l])
        hx = modulate(rms_norm(x, norm1_g[l]), sh1, sc1)
        yx, _, _ = mixer_sublayer(hx, kc, vc, rope, w_in[l], q_gain[l], k_gain[l],
                                  hy_short_w[l], hy_short_b[l], spec_x, hy_bias[l], w_branch[l], w_out[l])
        x = x + g1 * yx
        h2 = modulate(rms_norm(x, norm2_g[l]), sh2, sc2)
        x = x + g2 * expert_choice_moe(h2, w_router[l], w_gate[l], w_up[l], w_down[l])

        if not last:
            ctx = ctx + cg1 * yc
            hc2 = modulate(rms_norm(ctx, norm2_g[l]), csh2, csc2)
            ctx = ctx + cg2 * expert_choice_moe(hc2, w_router[l], w_gate[l], w_up[l], w_down[l])
    return rms_norm(x, final_g)


D_MIX = D_MODEL
MLA_HEADS = 4
MLA_NOPE = 128
MLA_ROPE = 64
MLA_V = 128
MLA_WIDTH = MLA_HEADS * MLA_V
Q_LORA = 256
KV_LORA = 128
RW_HEAD = 64
RW_WIDTH = D_MIX - MLA_WIDTH
RW_HEADS = RW_WIDTH // RW_HEAD
W_LORA = 64
A_LORA = 64
RW_GN_EPS = 64e-5
NORM_EPS = 1e-6
MLA_COLS = Q_LORA + KV_LORA + MLA_ROPE
RW_SHIFT_COLS = 3 * RW_WIDTH + W_LORA + A_LORA
GATE_COLS = D_MIX
D_IN = MLA_COLS + RW_SHIFT_COLS + GATE_COLS


def rmsnorm(x, g):
    xf = x.astype(jnp.float32)
    y = xf * lax.rsqrt(jnp.mean(xf * xf, axis=-1, keepdims=True) + NORM_EPS)
    return (y * g.astype(jnp.float32)).astype(x.dtype)

def rope_tables(positions):
    inv_freq = ROPE_THETA ** (-jnp.arange(0, MLA_ROPE, 2, dtype=jnp.float32) / MLA_ROPE)
    ang = positions.astype(jnp.float32)[..., None] * inv_freq
    ang = jnp.concatenate([ang, ang], axis=-1)
    return jnp.cos(ang), jnp.sin(ang)

def apply_rope_3(x, cos, sin):
    x1, x2 = jnp.split(x, 2, axis=-1)
    rot = jnp.concatenate([-x2, x1], axis=-1)
    return (x.astype(jnp.float32) * cos + rot.astype(jnp.float32) * sin).astype(x.dtype)

def token_shift(p):
    return jnp.pad(p[:, :-1], ((0, 0), (1, 0), (0, 0)))

def mla_attention(q_nope, q_rope, k_nope, k_rope, v):
    T = q_nope.shape[1]
    scale = (MLA_NOPE + MLA_ROPE) ** -0.5
    outs = []
    for i in range(T // Q_BLOCK):
        s, e = i * Q_BLOCK, (i + 1) * Q_BLOCK
        scores = (jnp.einsum('bqhd,bkhd->bhqk', q_nope[:, s:e], k_nope[:, :e])
                  + jnp.einsum('bqhr,bkr->bhqk', q_rope[:, s:e], k_rope[:, :e])).astype(jnp.float32) * scale
        mask = (s + jnp.arange(Q_BLOCK))[:, None] >= jnp.arange(e)[None, :]
        scores = jnp.where(mask, scores, -jnp.inf)
        probs = jax.nn.softmax(scores, axis=-1).astype(v.dtype)
        outs.append(jnp.einsum('bhqk,bkhd->bqhd', probs, v[:, :e]))
    return jnp.concatenate(outs, axis=1)

def wkv7_scan(r, w, k, v, kk, a):
    B, T, H, N = r.shape

    def step(S, inp):
        r_t, w_t, k_t, v_t, kk_t, a_t = inp
        sa = jnp.einsum('bhvk,bhk->bhv', S, -kk_t)
        S = (S * w_t[:, :, None, :] + sa[..., None] * (kk_t * a_t)[:, :, None, :]
             + v_t[..., None] * k_t[:, :, None, :])
        return S, jnp.einsum('bhvk,bhk->bhv', S, r_t)

    xs = tuple(jnp.moveaxis(t.astype(jnp.float32), 1, 0) for t in (r, w, k, v, kk, a))
    S0 = jnp.zeros((B, H, N, N), jnp.float32)
    _, ys = lax.scan(step, S0, xs)
    return jnp.moveaxis(ys, 0, 1)

def third_inputs(seed: int = 0) -> dict:
    key = jax.random.key(seed)
    ks = jax.random.split(key, 24)
    L = DEPTH
    f32 = jnp.float32

    def nrm(k, shape, scale):
        return jax.random.normal(k, shape, f32) * scale

    x = nrm(ks[0], (BATCH, SEQ, D_MODEL), 1.0)
    offset = jax.random.randint(ks[1], (BATCH, 1), 0, 4096, dtype=jnp.int32)
    positions = offset + jnp.arange(SEQ, dtype=jnp.int32)[None, :]
    return {
        'x': x,
        'positions': positions,
        'norm_pre_g': 1.0 + nrm(ks[2], (L, D_MODEL), 0.02),
        'w_in': nrm(ks[3], (L, D_MODEL, D_IN), D_MODEL ** -0.5),
        'mla_q_norm_g': 1.0 + nrm(ks[4], (L, Q_LORA), 0.02),
        'mla_w_uq': nrm(ks[5], (L, Q_LORA, MLA_HEADS * (MLA_NOPE + MLA_ROPE)), Q_LORA ** -0.5),
        'mla_kv_norm_g': 1.0 + nrm(ks[6], (L, KV_LORA), 0.02),
        'mla_w_ukv': nrm(ks[7], (L, KV_LORA, MLA_HEADS * (MLA_NOPE + MLA_V)), KV_LORA ** -0.5),
        'rw_mu': jax.random.uniform(ks[8], (L, RW_SHIFT_COLS), f32),
        'rw_w0': -2.5 + nrm(ks[9], (L, RW_WIDTH), 0.5),
        'rw_w2': nrm(ks[10], (L, W_LORA, RW_WIDTH), 0.5 * W_LORA ** -0.5),
        'rw_a0': nrm(ks[11], (L, RW_WIDTH), 0.1),
        'rw_a2': nrm(ks[12], (L, A_LORA, RW_WIDTH), 0.5 * A_LORA ** -0.5),
        'rw_k_k': 0.85 + nrm(ks[13], (L, RW_WIDTH), 0.05),
        'rw_k_a': 1.0 + nrm(ks[14], (L, RW_WIDTH), 0.05),
        'rw_r_k': nrm(ks[15], (L, RW_HEADS, RW_HEAD), 0.1),
        'rw_ln_g': 1.0 + nrm(ks[16], (L, RW_WIDTH), 0.02),
        'rw_ln_b': nrm(ks[17], (L, RW_WIDTH), 0.02),
        'w_out': nrm(ks[18], (L, D_MIX, D_MODEL), D_MIX ** -0.5),
        'norm_post_g': 1.0 + nrm(ks[19], (L, D_MODEL), 0.02),
    }

def third_block(x, positions, norm_pre_g, w_in, mla_q_norm_g, mla_w_uq, mla_kv_norm_g, mla_w_ukv,
              rw_mu, rw_w0, rw_w2, rw_a0, rw_a2, rw_k_k, rw_k_a, rw_r_k, rw_ln_g, rw_ln_b,
              w_out, norm_post_g):
    B, T, _ = x.shape
    f32 = jnp.float32
    cos, sin = rope_tables(positions)
    h = x
    for l in range(DEPTH):
        u = rmsnorm(h, norm_pre_g[l])
        p = u @ w_in[l]
        p_mla, p_rw, z = jnp.split(p, [MLA_COLS, MLA_COLS + RW_SHIFT_COLS], axis=-1)

        c_q, c_kv, k_r = jnp.split(p_mla, [Q_LORA, Q_LORA + KV_LORA], axis=-1)
        q = (rmsnorm(c_q, mla_q_norm_g[l]) @ mla_w_uq[l]).reshape(B, T, MLA_HEADS, MLA_NOPE + MLA_ROPE)
        q_nope, q_rope = jnp.split(q, [MLA_NOPE], axis=-1)
        kv = (rmsnorm(c_kv, mla_kv_norm_g[l]) @ mla_w_ukv[l]).reshape(B, T, MLA_HEADS, MLA_NOPE + MLA_V)
        k_nope, v_mla = jnp.split(kv, [MLA_NOPE], axis=-1)
        q_rope = apply_rope_3(q_rope, cos[:, :, None, :], sin[:, :, None, :])
        k_r = apply_rope_3(k_r, cos, sin)
        y_mla = mla_attention(q_nope, q_rope, k_nope, k_r, v_mla).reshape(B, T, MLA_WIDTH)

        ps = p_rw + (token_shift(p_rw) - p_rw) * rw_mu[l]
        r, k, v, xw, xa = jnp.split(
            ps, [RW_WIDTH, 2 * RW_WIDTH, 3 * RW_WIDTH, 3 * RW_WIDTH + W_LORA], axis=-1)
        w_log = -jax.nn.softplus(-(rw_w0[l] + jnp.tanh(xw) @ rw_w2[l]).astype(f32)) - 0.5
        decay = jnp.exp(-jnp.exp(w_log))
        a = jax.nn.sigmoid((rw_a0[l] + xa @ rw_a2[l]).astype(f32))
        kk = (k * rw_k_k[l]).astype(f32).reshape(B, T, RW_HEADS, RW_HEAD)
        kk = kk / jnp.maximum(jnp.linalg.norm(kk, axis=-1, keepdims=True), 1e-12)
        k = k.astype(f32) * (1.0 + (a - 1.0) * rw_k_a[l].astype(f32))
        heads = lambda t: t.reshape(B, T, RW_HEADS, RW_HEAD)
        r_h, k_h, v_h = heads(r.astype(f32)), heads(k), heads(v.astype(f32))
        y = wkv7_scan(r_h, heads(decay), k_h, v_h, kk, heads(a))
        mean = jnp.mean(y, axis=-1, keepdims=True)
        var = jnp.mean(jnp.square(y - mean), axis=-1, keepdims=True)
        y = ((y - mean) * lax.rsqrt(var + RW_GN_EPS)).reshape(B, T, RW_WIDTH)
        y = y * rw_ln_g[l].astype(f32) + rw_ln_b[l].astype(f32)
        bonus = jnp.sum(r_h * k_h * rw_r_k[l].astype(f32), axis=-1, keepdims=True) * v_h
        y_rw = (y + bonus.reshape(B, T, RW_WIDTH)).astype(x.dtype)

        y_cat = jnp.concatenate([y_mla, y_rw], axis=-1) * jax.nn.silu(z)
        out = y_cat @ w_out[l]
        h = h + rmsnorm(out, norm_post_g[l])
    return h


_first_inputs_3 = third_inputs


def third_inputs(seed=0):
    import zlib

    import numpy as np

    out = dict(_first_inputs_3(seed))
    spreads = {}
    factors = {'mla_q_norm_g': 8.0,
     'mla_kv_norm_g': 8.0,
     'rw_k_k': 3.5,
     'rw_ln_g': 4.163,
     'rw_ln_b': 4.303,
     'norm_post_g': 3.995}
    for name, (base, spread) in spreads.items():
        noise = np.random.default_rng([zlib.crc32(name.encode()), seed]).standard_normal(out[name].shape)
        drawn = base * np.exp(spread * noise) if base else spread * noise
        out[name] = __import__('jax').numpy.asarray(drawn.astype(out[name].dtype))
    for name, factor in factors.items():
        out[name] = (out[name] * factor).astype(out[name].dtype)
    return out


_narrow_inputs_3 = third_inputs


def third_inputs(seed=0):

    out = dict(_narrow_inputs_3(seed))
    wider = {'rw_w2': 3.23, 'rw_k_k': 5.88, 'rw_ln_g': 6.87, 'rw_ln_b': 6.98, 'norm_post_g': 3.28}
    for name, times in wider.items():
        mean = out[name].mean()
        out[name] = (mean + times * (out[name] - mean)).astype(out[name].dtype)
    return out


def setup_inputs(seed=0):
    out = dict(first_inputs(seed))
    for name, value in second_inputs(seed + 1).items():
        if name != "x":
            out[name + "_2"] = value
    for name, value in third_inputs(seed + 2).items():
        if name != "x":
            out[name + "_3"] = value
    return out


def reference(
    x, mem, g_in, w_in, conv_w, conv_b, g_mem, w_mem_kv, g_sb_out, g_conv_out, g_mem_out, w_out,
    g_final, c_2, ctx_2, c_ctx_2, w_mod_2, b_mod_2, norm1_g_2, norm2_g_2, w_in_2, q_gain_2,
    k_gain_2, hy_short_w_2, hy_short_b_2, hy_f_w1_2, hy_f_b1_2, hy_f_w2_2, hy_f_b2_2, hy_f_w3_2,
    hy_f_freq_2, hy_bias_2, w_branch_2, w_out_2, w_router_2, w_gate_2, w_up_2, w_down_2,
    final_g_2, positions_3, norm_pre_g_3, w_in_3, mla_q_norm_g_3, mla_w_uq_3, mla_kv_norm_g_3,
    mla_w_ukv_3, rw_mu_3, rw_w0_3, rw_w2_3, rw_a0_3, rw_a2_3, rw_k_k_3, rw_k_a_3, rw_r_k_3,
    rw_ln_g_3, rw_ln_b_3, w_out_3, norm_post_g_3,
):
    x = first_block(
        x, mem, g_in, w_in, conv_w, conv_b, g_mem, w_mem_kv, g_sb_out, g_conv_out, g_mem_out,
        w_out, g_final,
    )
    x = second_block(
        x, c_2, ctx_2, c_ctx_2, w_mod_2, b_mod_2, norm1_g_2, norm2_g_2, w_in_2, q_gain_2,
        k_gain_2, hy_short_w_2, hy_short_b_2, hy_f_w1_2, hy_f_b1_2, hy_f_w2_2, hy_f_b2_2,
        hy_f_w3_2, hy_f_freq_2, hy_bias_2, w_branch_2, w_out_2, w_router_2, w_gate_2, w_up_2,
        w_down_2, final_g_2,
    )
    return third_block(
        x, positions_3, norm_pre_g_3, w_in_3, mla_q_norm_g_3, mla_w_uq_3, mla_kv_norm_g_3,
        mla_w_ukv_3, rw_mu_3, rw_w0_3, rw_w2_3, rw_a0_3, rw_a2_3, rw_k_k_3, rw_k_a_3, rw_r_k_3,
        rw_ln_g_3, rw_ln_b_3, w_out_3, norm_post_g_3,
    )


_drawn_inputs = setup_inputs


def setup_inputs(seed=0):
    import zlib

    import numpy as np

    out = dict(_drawn_inputs(seed))
    spreads = {}
    factors = {'ctx_2': 8.0,
     'c_ctx_2': 4.371,
     'norm1_g_2': 7.047,
     'norm2_g_2': 7.163,
     'q_gain_2': 8.0,
     'k_gain_2': 8.0,
     'hy_short_b_2': 8.0,
     'hy_f_b1_2': 7.163,
     'hy_f_b2_2': 6.294,
     'hy_f_freq_2': 8.0}
    for name, (base, spread) in spreads.items():
        noise = np.random.default_rng([zlib.crc32(name.encode()), seed]).standard_normal(out[name].shape)
        drawn = base * np.exp(spread * noise) if base else spread * noise
        out[name] = jnp.asarray(drawn.astype(out[name].dtype))
    for name, factor in factors.items():
        out[name] = (out[name] * factor).astype(out[name].dtype)
    return out
```

```python
from contextlib import ExitStack

import numpy as np

import concourse.bass as bass
from concourse import mybir
from concourse.bass import ds

F32 = mybir.dt.float32
I32 = mybir.dt.int32
U32 = mybir.dt.uint32
ALU = mybir.AluOpType
ACT = mybir.ActivationFunctionType
AX = mybir.AxisListType
P = 128
T = 1024
HALF = 512
D = 1024
KD = D // P
EPS = 1e-6


class Phase:

    SEMS_KEPT = 90
    retired = []

    def __init__(self, nc, name):
        self.nc, self.name, self.ctx, self.sems = nc, name, ExitStack(), []

    def __enter__(self):
        self.ctx.__enter__()
        return self

    def __exit__(self, *e):
        self.ctx.__exit__(*e)
        Phase.retired += self.sems
        if len(Phase.retired) > Phase.SEMS_KEPT:
            self.nc.clear_and_free_semaphores(Phase.retired)
            self.nc.all_engine_barrier()
            Phase.retired = []

    def sb(self, name, shape, dt=F32):
        return self.ctx.enter_context(self.nc.sbuf_tensor(f"{self.name}_{name}", shape, dt))

    def ps(self, name, shape):
        return self.ctx.enter_context(self.nc.psum_tensor(f"{self.name}_{name}", shape, F32))

    def sem(self, name):
        self.sems.append(self.nc.alloc_semaphore(f"{self.name}_{name}"))
        return self.sems[-1]

    def block(self):
        return self.ctx.enter_context(self.nc.Block())


F32R = mybir.dt.float32r


def split_hi(nc, hi, x):
    return nc.vector.tensor_copy(hi, x)


def split_products(nc, out, w_hi, w_lo, x_hi, x_lo, start, stop):
    nc.tensor.matmul(out, w_hi, x_hi, start=start, stop=False)
    nc.tensor.matmul(out, w_hi, x_lo, start=False, stop=False)
    return nc.tensor.matmul(out, w_lo, x_hi, start=False, stop=stop)


def gemm_phase(nc, name, acts, w_dram, K, w_col0, n_cols, tokens=T, act_dram=None, out_dram=None, out_row0=0,
               residual=None, res_gain=None, copy_to=None):
    KC = K // P
    halves = [(h, min(HALF, tokens - h)) for h in range(0, tokens, HALF)]
    NH = len(halves)
    n_tiles, tail = n_cols // P, n_cols % P
    n_tiles += tail > 0
    full_pairs = (n_cols // P) // 2
    rest = [(n // 2, n % 2, min(P, n_cols - n * P)) for n in range(2 * full_pairs, n_tiles)]
    uses = [(n_tiles + 1) // 2, n_tiles // 2]
    first = [(0, s, P) for s in range(2)] if full_pairs else rest
    later = rest if full_pairs else []
    with Phase(nc, name) as ph:
        if act_dram is not None:
            acts = ph.sb("acts", [P, KC, tokens])
        acts_hi, acts_lo = ph.sb("acts_hi", [P, KC, tokens], F32R), ph.sb("acts_lo", [P, KC, tokens], F32R)
        w_sb = [ph.sb(f"w{s}", [P, KC, P]) for s in range(2)]
        w_hi = [ph.sb(f"w_hi{s}", [P, KC, P], F32R) for s in range(2)]
        w_lo = [ph.sb(f"w_lo{s}", [P, KC, P], F32R) for s in range(2)]
        out_sb = [ph.sb(f"out{s}", [P, tokens]) for s in range(2)]
        acc = [[ph.ps(f"acc{s}{h}", [P, HALF]) for h in range(NH)] for s in range(2)]
        acts_loaded, acts_hi_ready = ph.sem("acts_loaded"), ph.sem("acts_hi_ready")
        acts_lo_ready = [ph.sem(f"acts_lo_ready{b}") for b in range(2)]
        w_loaded = [ph.sem(f"w_loaded{s}") for s in range(2)]
        w_hi_ready, w_split = [ph.sem(f"w_hi_ready{s}") for s in range(2)], [ph.sem(f"w_split{s}") for s in range(2)]
        acc_ready = [ph.sem(f"acc_ready{s}") for s in range(2)]
        copied = [ph.sem(f"copied{s}") for s in range(2)]
        gained, pool_step, out_free = ph.sem("gained"), ph.sem("pool_step"), [ph.sem(f"out_free{s}") for s in range(2)]
        w_view = w_dram.rearrange("(c p) n -> p c n", p=P)
        block = ph.block()

        @block.sync
        def _(sp):
            def load(i, s, m=P):
                sp.dma_start(w_sb[s][:, :, 0:m], w_view[:, :, ds((i * 2 + s) * P + w_col0, m)]).then_inc(w_loaded[s], 16)

            for at in first[:2]:
                load(*at)
            if act_dram is not None:
                for c in range(KC):
                    sp.dma_start(acts[:, c, :], act_dram[c * P:(c + 1) * P, :]).then_inc(acts_loaded, 16)
            if full_pairs > 1:
                with sp.Fori(1, full_pairs) as i:
                    for s in range(2):
                        sp.wait_ge(w_split[s], i)
                        load(i, s)
            for i, s, m in later:
                sp.wait_ge(w_split[s], i)
                load(i, s, m)

        @block.vector
        def _(dve):
            def split(i, s, m=P, loop=False):
                dve.wait_ge(w_loaded[s], i * 16 + 16)
                if loop:
                    dve.wait_ge(acc_ready[s], i * NH)
                split_hi(nc, w_hi[s][:, :, 0:m], w_sb[s][:, :, 0:m]).then_inc(w_hi_ready[s], 1)
                dve.wait_ge(w_hi_ready[s], i + 1)
                nc.vector.tensor_tensor(w_lo[s][:, :, 0:m], w_sb[s][:, :, 0:m], w_hi[s][:, :, 0:m].bitcast(F32),
                                        ALU.subtract).then_inc(w_split[s], 1)

            split(*first[0])
            for c in range(KC):
                if act_dram is not None:
                    dve.wait_ge(acts_loaded, 16 * KC)
                split_hi(nc, acts_hi[:, c, :], acts[:, c, :]).then_inc(acts_hi_ready, 1)
                if c % 2 == 0:
                    dve.wait_ge(acts_hi_ready, c + 1)
                    nc.vector.tensor_tensor(acts_lo[:, c, :], acts[:, c, :], acts_hi[:, c, :].bitcast(F32),
                                            ALU.subtract).then_inc(acts_lo_ready[0], 1)
            for at in first[1:2]:
                split(*at)
            if full_pairs > 1:
                with dve.Fori(1, full_pairs) as i:
                    for s in range(2):
                        split(i, s, loop=True)
            for i, s, m in later:
                split(i, s, m, loop=True)

        @block.gpsimd
        def _(pool):
            for c in range(1, KC, 2):
                pool.wait_ge(acts_hi_ready, c + 1)
                nc.gpsimd.tensor_tensor(acts_lo[:, c, :], acts[:, c, :], acts_hi[:, c, :].bitcast(F32),
                                        ALU.subtract).then_inc(acts_lo_ready[1], 1)
            if residual is None:
                return

            def add(i, s):
                for h, (t0, tn) in enumerate(halves):
                    rows = residual[:, ds(i * 2 + s, 1), t0:t0 + tn]
                    part = out_sb[s][:, t0:t0 + tn].rearrange("p (o t) -> p o t", o=1)
                    pool.wait_ge(copied[s], i * NH + (NH + h + 1))
                    pool.sem_inc(pool_step, 1)
                    if res_gain is not None:
                        gain = res_gain[:, ds(i * 2 + s, 1)].rearrange("p (o t) -> p o t", o=1).to_broadcast([P, 1, tn])
                        nc.gpsimd.tensor_tensor(part, part, gain, ALU.mult).then_inc(gained, 1)
                        pool.wait_ge(gained, i * (2 * NH) + (NH * s + h + 1))
                        pool.sem_inc(pool_step, 1)
                    nc.gpsimd.tensor_tensor(rows, rows, part, ALU.add).then_inc(out_free[s], 16 // NH)

            with pool.Fori(0, full_pairs) as i:
                for s in range(2):
                    add(i, s)

        @block.tensor
        def _(pe):
            def tile(i, s, m=P, first_tile=False):
                pe.wait_ge(w_split[s], i + 1)
                pe.wait_ge(copied[s], i * NH + NH)
                for h, (t0, tn) in enumerate(halves):
                    for c in range(KC):
                        if first_tile and h == 0:
                            pe.wait_ge(acts_lo_ready[c % 2], c // 2 + 1)
                        mm = split_products(nc, acc[s][h][0:m, 0:tn], w_hi[s][:, c, 0:m], w_lo[s][:, c, 0:m],
                                            acts_hi[:, c, t0:t0 + tn], acts_lo[:, c, t0:t0 + tn],
                                            c == 0, c == KC - 1)
                    mm.then_inc(acc_ready[s], 1)

            for n, (i, s, m) in enumerate(first):
                tile(i, s, m, first_tile=(n == 0))
            if full_pairs > 1:
                with pe.Fori(1, full_pairs) as i:
                    for s in range(2):
                        tile(i, s)
            for i, s, m in later:
                tile(i, s, m)

        @block.scalar
        def _(act):
            def copy_out(i, s, m=P):
                act.wait_ge(out_free[s], i * 16 + 16)
                for h, (t0, tn) in enumerate(halves):
                    act.wait_ge(acc_ready[s], i * NH + (h + 1))
                    if copy_to is not None:
                        nc.scalar.activation(copy_to[:, ds(i * 2 + s, 1), t0:t0 + tn],
                                             acc[s][h][:, 0:tn].rearrange("p (o t) -> p o t", o=1),
                                             ACT.Copy).then_inc(copied[s], 1)
                    else:
                        nc.scalar.activation(out_sb[s][0:m, t0:t0 + tn], acc[s][h][0:m, 0:tn], ACT.Copy).then_inc(copied[s], 1)
                if out_dram is not None:
                    act.wait_ge(copied[s], i * NH + 2 * NH)
                    act.dma_start(out_dram[ds((i * 2 + s) * P + out_row0, m), :], out_sb[s][0:m, :]).then_inc(out_free[s], 16)

            for s in range(2):
                act.sem_inc(copied[s], NH)
                act.sem_inc(out_free[s], 16 if copy_to is None else 16 * uses[0] + 16)
            if full_pairs:
                with act.Fori(0, full_pairs) as i:
                    for s in range(2):
                        copy_out(i, s)
            for i, s, m in rest:
                copy_out(i, s, m)
            if out_dram is not None:
                for s in range(2):
                    act.wait_ge(out_free[s], 16 * uses[s] + 16)


def stream_gemm_phase(nc, name, w_dram, act_dram, out_dram):
    KC, N = act_dram.shape[0] // P, w_dram.shape[1]
    NT = N // P
    RING = 4
    with Phase(nc, name) as ph:
        x_sb = [ph.sb(f"x{r}", [P, T]) for r in range(RING)]
        w_sb = [ph.sb(f"w{r}", [P, N]) for r in range(RING)]
        x_part = [[ph.sb(f"x_{n}{s}", [P, T], F32R) for n in ("hi", "lo")] for s in range(2)]
        w_part = [[ph.sb(f"w_{n}{s}", [P, N], F32R) for n in ("hi", "lo")] for s in range(2)]
        out_sb = [ph.sb(f"out{n}", [P, T]) for n in range(NT)]
        acc = [[ph.ps(f"acc{n}{h}", [P, HALF]) for h in range(2)] for n in range(NT)]
        loaded = [ph.sem(f"loaded{r}") for r in range(RING)]
        hi_ready, w_lo_ready = ph.sem("hi_ready"), ph.sem("w_lo_ready")
        x_lo_ready = [ph.sem(f"x_lo_ready{h}") for h in range(2)]
        summed, copied, stored = ph.sem("summed"), ph.sem("copied"), ph.sem("stored")
        block = ph.block()

        @block.sync
        def _(sp):
            for c in range(KC):
                r = c % RING
                if c >= RING:
                    sp.wait_ge(w_lo_ready, c - RING + 1)
                    for h in range(2):
                        sp.wait_ge(x_lo_ready[h], c - RING + 1)
                sp.dma_start(w_sb[r][:, :], w_dram[c * P:(c + 1) * P, :]).then_inc(loaded[r], 16)
                sp.dma_start(x_sb[r][:, :], act_dram[c * P:(c + 1) * P, :]).then_inc(loaded[r], 16)
            for n in range(NT):
                sp.wait_ge(copied, 2 * n + 2)
                sp.dma_start(out_dram[n * P:(n + 1) * P, :], out_sb[n][:, :]).then_inc(stored, 16)
            sp.wait_ge(stored, 16 * NT)

        @block.vector
        def _(dve):
            for c in range(KC):
                r, s = c % RING, c % 2
                dve.wait_ge(loaded[r], 32 * (c // RING + 1))
                if c >= 2:
                    dve.wait_ge(summed, c - 1)
                split_hi(nc, w_part[s][0][:, :], w_sb[r][:, :]).then_inc(hi_ready, 1)
                split_hi(nc, x_part[s][0][:, :], x_sb[r][:, :]).then_inc(hi_ready, 1)
                dve.wait_ge(hi_ready, 2 * c + 2)
                nc.vector.tensor_tensor(w_part[s][1][:, :], w_sb[r][:, :], w_part[s][0][:, :].bitcast(F32),
                                        ALU.subtract).then_inc(w_lo_ready, 1)
                nc.vector.tensor_tensor(x_part[s][1][:, 0:HALF], x_sb[r][:, 0:HALF], x_part[s][0][:, 0:HALF].bitcast(F32),
                                        ALU.subtract).then_inc(x_lo_ready[0], 1)

        @block.gpsimd
        def _(pool):
            for c in range(KC):
                r, s = c % RING, c % 2
                pool.wait_ge(hi_ready, 2 * c + 2)
                nc.gpsimd.tensor_tensor(x_part[s][1][:, HALF:T], x_sb[r][:, HALF:T], x_part[s][0][:, HALF:T].bitcast(F32),
                                        ALU.subtract).then_inc(x_lo_ready[1], 1)

        @block.tensor
        def _(pe):
            for c in range(KC):
                s = c % 2
                pe.wait_ge(w_lo_ready, c + 1)
                for n in range(NT):
                    for h in range(2):
                        if n == 0:
                            pe.wait_ge(x_lo_ready[h], c + 1)
                        mm = split_products(nc, acc[n][h][:, :], w_part[s][0][:, n * P:(n + 1) * P],
                                            w_part[s][1][:, n * P:(n + 1) * P], x_part[s][0][:, h * HALF:(h + 1) * HALF],
                                            x_part[s][1][:, h * HALF:(h + 1) * HALF], c == 0, c == KC - 1)
                mm.then_inc(summed, 1)

        @block.scalar
        def _(act):
            act.wait_ge(summed, KC)
            for n in range(NT):
                for h in range(2):
                    nc.scalar.activation(out_sb[n][:, h * HALF:(h + 1) * HALF], acc[n][h][:, :], ACT.Copy).then_inc(copied, 1)


def transpose_phase(nc, name, ident, src_dram, dst, tokens):
    KC = src_dram.shape[1] // P
    NB = KC // 4
    pairs = tokens // P // 2
    with Phase(nc, name) as ph:
        rows = [ph.sb(f"rows{s}", [P, KC * P]) for s in range(2)]
        turned = [[ph.ps(f"turned{s}{b}", [P, 4, P]) for b in range(NB)] for s in range(2)]
        rows_loaded = [ph.sem(f"rows_loaded{s}") for s in range(2)]
        turned_ready = [ph.sem(f"turned_ready{s}") for s in range(2)]
        copied = [ph.sem(f"copied{s}") for s in range(2)]
        block = ph.block()

        @block.sync
        def _(sp):
            def load(i, s):
                sp.dma_start(rows[s][:, :], src_dram[ds((i * 2 + s) * P, P), :]).then_inc(rows_loaded[s], 16)

            for s in range(2):
                load(0, s)
            if pairs > 1:
                with sp.Fori(1, pairs) as i:
                    for s in range(2):
                        sp.wait_ge(turned_ready[s], i * NB)
                        load(i, s)

        @block.tensor
        def _(pe):
            with pe.Fori(0, pairs) as i:
                for s in range(2):
                    pe.wait_ge(rows_loaded[s], i * 16 + 16)
                    pe.wait_ge(copied[s], i * NB + NB)
                    for b in range(NB):
                        for c in range(4):
                            tr = nc.tensor.transpose(turned[s][b][:, c, :], rows[s][:, (4 * b + c) * P:(4 * b + c + 1) * P],
                                                     ident[:, :])
                        tr.then_inc(turned_ready[s], 1)

        @block.vector
        def _(dve):
            for s in range(2):
                dve.sem_inc(copied[s], NB)
            with dve.Fori(0, pairs) as i:
                for s in range(2):
                    for b in range(NB):
                        dve.wait_ge(turned_ready[s], i * NB + (b + 1))
                        nc.vector.tensor_copy(dst[:, 4 * b:4 * b + 4, ds((i * 2 + s) * P, P)],
                                              turned[s][b][:, :, :]).then_inc(copied[s], 1)


def norm_phase(nc, name, sum_matrix, src, dst, groups, g_vecs, tokens=T, scale_cols=None, shift_cols=None, src_dram=None,
               store_dram=None, eps=EPS, bound=ALU.add):
    chunks = [c for g, _ in groups for c in g]
    KC = len(chunks)
    halves = [(h, min(HALF, tokens - h)) for h in range(0, tokens, HALF)]
    with Phase(nc, name) as ph:
        gain = ph.sb("gain", [P, KC])
        square = [ph.sb(f"square{s}", [P, HALF]) for s in range(2)]
        root = [ph.sb(f"root{s}", [P, HALF]) for s in range(2)]
        inv = [ph.sb(f"inv{s}", [P, HALF]) for s in range(2)]
        sums = [ph.ps(f"sums{s}", [P, HALF]) for s in range(2)]
        src_loaded, gain_loaded, gain_ready = ph.sem("src_loaded"), ph.sem("gain_loaded"), ph.sem("gain_ready")
        square_ready, square_used, mean_ready = ph.sem("square_ready"), ph.sem("square_used"), ph.sem("mean_ready")
        root_ready, inv_ready, scaled, shifted = ph.sem("root_ready"), ph.sem("inv_ready"), ph.sem("scaled"), ph.sem("shifted")
        stored = ph.sem("stored")
        block = ph.block()
        n_gain = sum((1 if v.shape[0] == P else 2) for v in g_vecs) if g_vecs else 0
        steps = [(h, g) for h in range(len(halves)) for g in range(len(groups))]

        @block.sync
        def _(sp):
            if src_dram is not None:
                for c in range(KC):
                    sp.dma_start(src[:, c, :], src_dram[c]).then_inc(src_loaded, 16)
            if g_vecs:
                for c, v in enumerate(g_vecs):
                    if v.shape[0] == P:
                        sp.dma_start(gain[:, c:c + 1], v.rearrange("(p o) -> p o", o=1)).then_inc(gain_loaded, 16)
                    else:
                        for b in range(2):
                            sp.dma_start(gain[64 * b:64 * b + 64, c:c + 1],
                                         v.rearrange("(p o) -> p o", o=1)).then_inc(gain_loaded, 16)
            if store_dram is not None:
                done = len(halves) * KC
                sp.wait_ge(shifted if shift_cols is not None else scaled, done)
                for c in range(KC):
                    sp.dma_start(store_dram[c], dst[:, c, :]).then_inc(stored, 16)
                sp.wait_ge(stored, 16 * KC)

        @block.scalar
        def _(act):
            if src_dram is not None:
                act.wait_ge(src_loaded, 16 * KC)
            n = 0
            for k, (h, g) in enumerate(steps):
                t0, tn = halves[h]
                for c in groups[g][0]:
                    if n >= 2:
                        act.wait_ge(square_used, n - 1)
                    nc.scalar.activation(square[n % 2][:, 0:tn], src[:, c, t0:t0 + tn], ACT.Square).then_inc(square_ready, 1)
                    n += 1
                act.wait_ge(mean_ready, k + 1)
                nc.scalar.activation(root[k % 2][:, 0:tn], root[k % 2][:, 0:tn], ACT.Sqrt).then_inc(root_ready, 1)
            if shift_cols is not None:
                n = 0
                for h, g in steps:
                    t0, tn = halves[h]
                    for c in groups[g][0]:
                        act.wait_ge(scaled, n + 1)
                        nc.scalar.activation(dst[:, c, t0:t0 + tn], dst[:, c, t0:t0 + tn], ACT.Identity,
                                             bias=shift_cols[:, c:c + 1]).then_inc(shifted, 1)
                        n += 1

        @block.tensor
        def _(pe):
            n = 0
            for k, (h, g) in enumerate(steps):
                t0, tn = halves[h]
                if k >= 2:
                    pe.wait_ge(mean_ready, k - 1)
                for j, c in enumerate(groups[g][0]):
                    pe.wait_ge(square_ready, n + 1)
                    nc.tensor.matmul(sums[k % 2][:, 0:tn], sum_matrix[:, :], square[n % 2][:, 0:tn], start=(j == 0),
                                     stop=(j == len(groups[g][0]) - 1)).then_inc(square_used, 1)
                    n += 1

        @block.vector
        def _(dve):
            if g_vecs:
                dve.wait_ge(gain_loaded, 16 * n_gain)
            if src_dram is not None:
                dve.wait_ge(src_loaded, 16 * KC)
            if scale_cols is not None:
                nc.vector.scalar_tensor_tensor(out=gain[:, :], in0=scale_cols, scalar=1.0, in1=gain[:, :],
                                               op0=ALU.add, op1=ALU.mult).then_inc(gain_ready, 1)
                dve.wait_ge(gain_ready, 1)
            n = 0

            def finish(k):
                nonlocal n
                h, g = steps[k]
                t0, tn = halves[h]
                dve.wait_ge(root_ready, k + 1)
                nc.vector.reciprocal(inv[k % 2][:, 0:tn], root[k % 2][:, 0:tn]).then_inc(inv_ready, 1)
                dve.wait_ge(inv_ready, k + 1)
                for c in groups[g][0]:
                    if g_vecs:
                        nc.vector.scalar_tensor_tensor(out=dst[:, c, t0:t0 + tn], in0=src[:, c, t0:t0 + tn], scalar=gain[:, c:c + 1],
                                                       in1=inv[k % 2][:, 0:tn], op0=ALU.mult, op1=ALU.mult).then_inc(scaled, 1)
                    else:
                        nc.vector.tensor_tensor(dst[:, c, t0:t0 + tn], src[:, c, t0:t0 + tn], inv[k % 2][:, 0:tn],
                                                ALU.mult).then_inc(scaled, 1)
                    n += 1

            m = 0
            for k, (h, g) in enumerate(steps):
                t0, tn = halves[h]
                m += len(groups[g][0])
                dve.wait_ge(square_used, m)
                nc.vector.tensor_scalar(root[k % 2][:, 0:tn], sums[k % 2][:, 0:tn], 1.0 / groups[g][1], eps,
                                        ALU.mult, bound).then_inc(mean_ready, 1)
                if k >= 1:
                    finish(k - 1)
            finish(len(steps) - 1)


def load_columns(eng, dst, vec, sem):
    eng.dma_start(dst, vec.rearrange("(c p) -> p c", p=P), allow_slow_non_contiguous=True).then_inc(sem, 16)


def attend_phase(nc, name, ident, n_heads, parts, v_src, out_dram, out_row0, dv, nk, scale, causal_mask=None):
    NQ, NB = T // P, nk // P
    TILES = 2 * NQ
    tiles = [(s, i) for s in range(2) for i in range(NQ)]

    def v0(s):
        return s * dv if dv < P else 0

    def blocks(i):
        return i + 1 if causal_mask is not None else NB

    with Phase(nc, name) as ph:
        q_sb = [[ph.sb(f"q{s}_{n}", [P, T]) for n in range(len(parts))] for s in range(2)]
        narrow = [width < P for width, _, _ in parts]
        k_one = [ph.sb(f"k_{n}", [P, nk]) if narrow[n] else None for n in range(len(parts))]
        k_sb = [[k_one[n] or ph.sb(f"k{s}_{n}", [P, nk]) for n in range(len(parts))] for s in range(2)]
        v_one = dv < P
        vT_sb = [ph.sb(f"vT{s}", [P, nk]) for s in range(1 if v_one else 2)]
        v_sb = [ph.sb(f"v{s}", [P, NB, P]) for s in range(1 if v_one else 2)]
        if v_one:
            vT_sb, v_sb = vT_sb * 2, v_sb * 2
        probs = [ph.sb(f"probs{b}", [P, nk]) for b in range(2)]
        probsT = [ph.sb(f"probsT{b}", [P, NB, P]) for b in range(2)]
        out_sb = [ph.sb(f"out{s}", [P, T]) for s in range(2)]
        top, neg_top = [ph.sb(f"top{b}", [P, 1]) for b in range(2)], [ph.sb(f"neg_top{b}", [P, 1]) for b in range(2)]
        total, inv = [ph.sb(f"total{b}", [P, 1]) for b in range(2)], [ph.sb(f"inv{b}", [P, 1]) for b in range(2)]
        NSB = -(-nk // HALF)
        scores = ph.ps("scores", [P, NSB * HALF])
        turned = ph.ps("turned", [P, NSB * 4, P])
        o_ps = [ph.ps(f"o{h}", [P, HALF]) for h in range(2)]
        loaded = [ph.sem(f"loaded{s}") for s in range(2)]
        v_turned, v_ready = ph.sem("v_turned"), ph.sem("v_ready")
        scores_ready, top_ready, neg_ready = ph.sem("scores_ready"), ph.sem("top_ready"), ph.sem("neg_ready")
        probs_ready, inv_ready, divided = ph.sem("probs_ready"), ph.sem("inv_ready"), ph.sem("divided")
        turned_ready, turned_copied, o_ready = ph.sem("turned_ready"), ph.sem("turned_copied"), ph.sem("o_ready")
        o_copied, stored = ph.sem("o_copied"), [ph.sem(f"stored{s}") for s in range(2)]
        zeroed = ph.sem("zeroed")
        v_turns = [0] if v_one else [0, NQ - 1]
        block = ph.block()
        NL = 2 * len(parts) + 1
        pairs = n_heads // 2

        @block.sync
        def _(sp):
            def load(pair, s):
                for n, (width, q_rows, k_rows) in enumerate(parts):
                    p0 = s * 64 if narrow[n] else 0
                    sp.dma_start(q_sb[s][n][p0:p0 + width, :], q_rows(pair, s)).then_inc(loaded[s], 16)
                    sp.dma_start(k_sb[s][n][p0:p0 + width, :], k_rows(pair, s)).then_inc(loaded[s], 16)
                p0 = s * 64 if v_one else 0
                sp.dma_start(vT_sb[s][p0:p0 + dv, :], v_src(pair, s)).then_inc(loaded[s], 16)

            for s in range(2):
                load(0, s)
            if pairs > 1:
                with sp.Fori(1, pairs) as pair:
                    sp.wait_ge(scores_ready, pair * TILES)
                    for s in range(2):
                        load(pair, s)

        @block.tensor
        def _(pe):
            if any(narrow):
                pe.wait_ge(zeroed, 2 * sum(narrow))
            with pe.Fori(0, pairs) as pair:
                def score(j):
                    s, i = tiles[j]
                    if j == 0:
                        for x in range(2):
                            pe.wait_ge(loaded[x], pair * (16 * NL) + 16 * NL)
                    if i == 0 and (s == 0 or not v_one):
                        if s == 1:
                            pe.wait_ge(turned_copied, pair * TILES + (j - 1))
                        for b in range(NB):
                            tr = nc.tensor.transpose(turned[:, b, :], vT_sb[s][:, b * P:(b + 1) * P], ident[:, :])
                        tr.then_inc(v_turned, 1)
                    if j >= 1:
                        pe.wait_ge(probs_ready, pair * TILES + j)
                    nb = blocks(i)
                    for b0 in range(0, nb, 4):
                        bn = min(4, nb - b0)
                        diagonal = causal_mask is not None and b0 + bn == nb
                        for n in range(len(parts)):
                            mm = nc.tensor.matmul(scores[:, b0 * P:(b0 + bn) * P],
                                                  q_sb[s][n][:, i * P:(i + 1) * P],
                                                  k_sb[s][n][:, b0 * P:(b0 + bn) * P],
                                                  start=(n == 0), stop=(n == len(parts) - 1 and not diagonal))
                        if diagonal:
                            mm = nc.tensor.matmul(scores[:, (nb - 1) * P:nb * P], ident[:, :], causal_mask[:, :],
                                                  start=False, stop=True)
                    mm.then_inc(scores_ready, 1)

                def turn(j):
                    s, i = tiles[j]
                    pe.wait_ge(divided, pair * TILES + (j + 1))
                    if j >= 1:
                        pe.wait_ge(turned_copied, pair * TILES + j)
                    if j in v_turns:
                        pe.wait_ge(v_ready, pair * len(v_turns) + (v_turns.index(j) + 1))
                    for b in range(blocks(i)):
                        tr = nc.tensor.transpose(turned[:, b, :], probs[j % 2][:, b * P:(b + 1) * P], ident[:, :])
                    tr.then_inc(turned_ready, 1)

                def product(j):
                    s, i = tiles[j]
                    pe.wait_ge(turned_copied, pair * TILES + (j + 1))
                    if i % 4 == 0 and j >= 8:
                        pe.wait_ge(o_copied, pair * 4 + (j // 4 - 1))
                    for b in range(blocks(i)):
                        mm = nc.tensor.matmul(o_ps[i // 4][0:dv, (i % 4) * P:(i % 4 + 1) * P], v_sb[s][:, b, v0(s):v0(s) + dv],
                                              probsT[j % 2][:, b, :], start=(b == 0), stop=(b == blocks(i) - 1))
                    mm.then_inc(o_ready, 1)

                for j in range(TILES + 2):
                    if j < TILES:
                        score(j)
                    if 1 <= j <= TILES:
                        turn(j - 1)
                    if j >= 2:
                        product(j - 2)
                pe.wait_ge(o_copied, pair * 4 + 4)

        @block.vector
        def _(dve):
            with dve.Fori(0, pairs) as pair:
                def inverse(j):
                    dve.wait_ge(probs_ready, pair * TILES + (j + 1))
                    nc.vector.reciprocal(inv[j % 2][:, :], total[j % 2][:, :]).then_inc(inv_ready, 1)

                def maximum(j):
                    s, i = tiles[j]
                    if i == 0 and (s == 0 or not v_one):
                        dve.wait_ge(v_turned, pair * len(v_turns) + (s + 1))
                        nc.vector.tensor_copy(v_sb[s][:, :, :], turned[:, 0:NB, :]).then_inc(v_ready, 1)
                    dve.wait_ge(scores_ready, pair * TILES + (j + 1))
                    nc.vector.reduce_max(top[j % 2][:, :], scores[:, 0:blocks(i) * P], AX.X).then_inc(top_ready, 1)
                    dve.wait_ge(top_ready, pair * TILES + (j + 1))
                    nc.vector.tensor_scalar(neg_top[j % 2][:, :], top[j % 2][:, :], -scale, None, ALU.mult).then_inc(neg_ready, 1)

                def copy(j):
                    s, i = tiles[j]
                    dve.wait_ge(turned_ready, pair * TILES + (j + 1))
                    if j >= 2:
                        dve.wait_ge(o_ready, pair * TILES + (j - 1))
                    nc.vector.tensor_copy(probsT[j % 2][:, 0:blocks(i), :], turned[:, 0:blocks(i), :]).then_inc(turned_copied, 1)

                for j in range(TILES + 1):
                    if j >= 1:
                        inverse(j - 1)
                    if j < TILES:
                        maximum(j)
                    if j >= 1:
                        copy(j - 1)

        @block.scalar
        def _(act):
            for s in range(2):
                act.sem_inc(stored[s], 16)
            with act.Fori(0, pairs) as pair:
                def leave(g):
                    s, h = g // 2, g % 2
                    act.wait_ge(o_ready, pair * TILES + 4 * (g + 1))
                    if h == 0:
                        act.wait_ge(stored[s], pair * 16 + 16)
                    nc.scalar.activation(out_sb[s][0:dv, h * HALF:(h + 1) * HALF], o_ps[h][0:dv, :], ACT.Copy).then_inc(o_copied, 1)
                    if h == 1:
                        act.wait_ge(o_copied, pair * 4 + (g + 1))
                        act.dma_start(out_dram[ds((pair * 2 + s) * dv + out_row0, dv), :], out_sb[s][0:dv, :]).then_inc(stored[s], 16)

                for j in range(TILES + 2):
                    if j < TILES:
                        act.wait_ge(neg_ready, pair * TILES + (j + 1))
                        if j >= 2:
                            act.wait_ge(turned_ready, pair * TILES + (j - 1))
                        n = blocks(tiles[j][1]) * P
                        nc.scalar.activation(probs[j % 2][:, 0:n], scores[:, 0:n], ACT.Exp, bias=neg_top[j % 2][:, :],
                                             scale=scale, accum_out=total[j % 2][:, :]).then_inc(probs_ready, 1)
                        act.wait_ge(inv_ready, pair * TILES + (j + 1))
                        nc.scalar.activation(probs[j % 2][:, 0:n], probs[j % 2][:, 0:n], ACT.Copy,
                                             scale=inv[j % 2][:, :]).then_inc(divided, 1)
                    if j >= 5 and (j - 5) % 4 == 0:
                        leave((j - 5) // 4)
            for s in range(2):
                act.wait_ge(stored[s], 16 * pairs + 16)

        @block.gpsimd
        def _(pool):
            for n in range(len(parts)):
                if narrow[n]:
                    for s in range(2):
                        h = 64 * (1 - s)
                        nc.gpsimd.memset(q_sb[s][n][h:h + 64, :], 0.0).then_inc(zeroed, 1)


def stick_phase(nc, name, ident, strict, neg_future, neg_upper, neg_ones, qT, kT, vT, out_dram, n_heads):
    pairs = n_heads // 2
    groups = [(s, h) for s in range(2) for h in range(2)]
    steps = [(g, kt) for g, (s, h) in enumerate(groups) for kt in reversed(range(4 * h + 4))]
    NS = len(steps)
    ends = [max(j for j in range(NS) if steps[j][0] == g) for g in range(4)]

    def col0(j):
        g, kt = steps[j]
        return max(0, kt - 4 * groups[g][1]) * P

    def diagonal(j):
        g, kt = steps[j]
        return kt >= 4 * groups[g][1]

    def first(j):
        return j == 0 or steps[j - 1][0] != steps[j][0]

    diagonals = [sum(diagonal(x) for x in range(j + 1)) for j in range(NS)]
    with Phase(nc, name) as ph:
        q_sb = [ph.sb(f"q{s}", [P, T]) for s in range(2)]
        k_sb = ph.sb("k", [P, T])
        vT_sb = ph.sb("vT", [P, T])
        v_sb = ph.sb("v", [P, T // P, P])
        log_term = [ph.sb(f"log_term{b}", [P, HALF]) for b in range(2)]
        softplus = [ph.sb(f"softplus{b}", [P, HALF]) for b in range(3)]
        later = [ph.sb(f"later{b}", [P, HALF]) for b in range(3)]
        zeros = ph.sb("zeros", [P, HALF])
        weights = [ph.sb(f"weights{b}", [P, HALF]) for b in range(2)]
        out_sb = [ph.sb(f"out{s}", [64, T]) for s in range(2)]
        z_ps = [ph.ps(f"z{b}", [P, HALF]) for b in range(4)]
        o_ps = [ph.ps(f"o{b}", [64, HALF]) for b in range(2)]
        v_ps = ph.ps("v_turned", [P, T // P, P])
        zeroed, loaded, scaled = ph.sem("zeroed"), ph.sem("loaded"), ph.sem("scaled")
        v_turned, v_ready = ph.sem("v_was_turned"), ph.sem("v_ready")
        z_ready, abs_ready, exp_ready, log_ready = ph.sem("z_ready"), ph.sem("abs_ready"), ph.sem("exp_ready"), ph.sem("log_ready")
        sp_made, sp_ready, later_ready = ph.sem("sp_made"), ph.sem("sp_ready"), ph.sem("later_ready")
        exponent_ready, weights_ready, o_ready = ph.sem("exponent_ready"), ph.sem("weights_ready"), ph.sem("o_ready")
        o_copied, stored = ph.sem("o_copied"), [ph.sem(f"stored{s}") for s in range(2)]
        block = ph.block()
        NL = 4

        @block.sync
        def _(sp):
            def load(pair):
                for s in range(2):
                    sp.dma_start(q_sb[s][64 * s:64 * s + 64, :], qT[ds((pair * 2 + s) * 64, 64), :]).then_inc(loaded, 16)
                sp.dma_start(k_sb[:, :], kT[ds(pair * P, P), :]).then_inc(loaded, 16)
                sp.dma_start(vT_sb[:, :], vT[ds(pair * P, P), :]).then_inc(loaded, 16)

            load(0)
            with sp.Fori(1, pairs) as pair:
                sp.wait_ge(z_ready, pair * NS)
                load(pair)

        @block.gpsimd
        def _(pool):
            for s in range(2):
                h = 64 * (1 - s)
                nc.gpsimd.memset(q_sb[s][h:h + 64, :], 0.0).then_inc(zeroed, 1)
            pool.wait_ge(zeroed, 2)
            nc.gpsimd.memset(zeros[:, :], 0.0).then_inc(zeroed, 1)
            pool.wait_ge(zeroed, 3)
            pool.sem_inc(later_ready, 1)
            with pool.Fori(0, pairs) as pair:
                for j in range(NS):
                    c0, old = col0(j), P * diagonal(j)
                    pool.wait_ge(sp_ready, pair * NS + (j + 1))
                    pool.wait_ge(later_ready, pair * NS + (j + 1))
                    if j >= 2:
                        pool.wait_ge(exponent_ready, pair * NS + (j - 1))
                    if old or first(j):
                        end = HALF if first(j) else c0 + P
                        cp = nc.gpsimd.tensor_tensor(later[j % 3][:, c0:end], softplus[j % 3][:, c0:end],
                                                     zeros[:, c0:end], ALU.add)
                        c0 = end
                    if c0 < HALF:
                        cp = nc.gpsimd.tensor_tensor(later[j % 3][:, c0:], later[(j - 1) % 3][:, c0:], softplus[j % 3][:, c0:], ALU.add)
                    cp.then_inc(later_ready, 1)

        @block.tensor
        def _(pe):
            pe.wait_ge(zeroed, 3)
            with pe.Fori(0, pairs) as pair:
                def score(j):
                    g, kt = steps[j]
                    s, h = groups[g]
                    if j == 0:
                        pe.wait_ge(scaled, pair * 2 + 2)
                        for b in range(T // P):
                            tr = nc.tensor.transpose(v_ps[:, b, :], vT_sb[:, b * P:(b + 1) * P], ident[:, :])
                        tr.then_inc(v_turned, 1)
                    if j >= 4:
                        pe.wait_ge(weights_ready, pair * NS + (j - 3))
                    c0 = col0(j)
                    nc.tensor.matmul(z_ps[j % 4][:, c0:], k_sb[:, kt * P:(kt + 1) * P], q_sb[s][:, h * HALF + c0:(h + 1) * HALF],
                                     start=True, stop=True).then_inc(z_ready, 1)

                def exponent(j):
                    c0 = col0(j)
                    pe.wait_ge(sp_ready, pair * NS + (j + 1))
                    if diagonal(j):
                        nc.tensor.matmul(z_ps[j % 4][:, c0:c0 + P], ident[:, :], neg_future[:, :], start=False, stop=False,
                                         skip_group_check=True)
                    if not first(j):
                        l0 = col0(j - 1)
                        pe.wait_ge(later_ready, pair * NS + (j + 1))
                        nc.tensor.matmul(z_ps[j % 4][:, l0:], neg_ones[:, :], later[(j - 1) % 3][:, l0:], start=False, stop=False,
                                         skip_group_check=True)
                    nc.tensor.matmul(z_ps[j % 4][:, c0:], neg_upper[:, :], softplus[j % 3][:, c0:], start=False,
                                     stop=True, skip_group_check=True).then_inc(exponent_ready, 1)

                def product(j):
                    g, kt = steps[j]
                    s, h = groups[g]
                    if j == 0:
                        pe.wait_ge(v_ready, pair + 1)
                    if first(j) and g >= 2:
                        pe.wait_ge(o_copied, pair * 4 + (g - 1))
                    pe.wait_ge(weights_ready, pair * NS + (j + 1))
                    mm = nc.tensor.matmul(o_ps[g % 2][:, col0(j):], v_sb[:, kt, s * 64:s * 64 + 64], weights[j % 2][:, col0(j):],
                                          start=first(j), stop=(kt == 0), skip_group_check=True)
                    mm.then_inc(o_ready, 1)

                for j in range(NS + 3):
                    if j < NS:
                        score(j)
                    if 2 <= j < NS + 2:
                        exponent(j - 2)
                    if 3 <= j:
                        product(j - 3)
                pe.wait_ge(o_copied, pair * 4 + 4)
                pe.wait_ge(later_ready, pair * NS + (NS + 1))

        @block.vector
        def _(dve):
            with dve.Fori(0, pairs) as pair:
                for j in range(NS + 1):
                    if j < NS:
                        if j == 0:
                            dve.wait_ge(v_turned, pair + 1)
                            nc.vector.tensor_copy(v_sb[:, :, :], v_ps[:, :, :]).then_inc(v_ready, 1)
                    if j >= 1:
                        i = j - 1
                        c0 = col0(i)
                        dve.wait_ge(log_ready, pair * NS + (i + 1))
                        if i >= 3:
                            dve.wait_ge(exponent_ready, pair * NS + (i - 2))
                            dve.wait_ge(later_ready, pair * NS + (i - 1))
                        sp = nc.vector.scalar_tensor_tensor(out=softplus[i % 3][:, c0:], in0=z_ps[i % 4][:, c0:], scalar=0.0,
                                                            in1=log_term[i % 2][:, c0:], op0=ALU.max, op1=ALU.add)
                        if diagonal(i):
                            sp.then_inc(sp_made, 1)
                            dve.wait_ge(sp_made, pair * diagonals[-1] + diagonals[i])
                            sp = nc.vector.tensor_tensor(softplus[i % 3][:, c0:c0 + P], softplus[i % 3][:, c0:c0 + P],
                                                         strict[:, :], ALU.mult)
                        sp.then_inc(sp_ready, 1)

        @block.scalar
        def _(act):
            for s in range(2):
                act.sem_inc(stored[s], 16)
            act.preload_act_table_set("natural_log_exp_and_others")
            act.wait_ge(zeroed, 2)
            with act.Fori(0, pairs) as pair:
                act.wait_ge(loaded, pair * (16 * NL) + 16 * NL)
                for s in range(2):
                    nc.scalar.activation(q_sb[s][:, :], q_sb[s][:, :], ACT.Copy, scale=64 ** -0.5).then_inc(scaled, 1)
                for j in range(NS + 3):
                    if j < NS:
                        c0 = col0(j)
                        act.wait_ge(z_ready, pair * NS + (j + 1))
                        if j >= 2:
                            act.wait_ge(sp_ready, pair * NS + (j - 1))
                        nc.scalar.activation(log_term[j % 2][:, c0:], z_ps[j % 4][:, c0:], ACT.Abs).then_inc(abs_ready, 1)
                        act.wait_ge(abs_ready, pair * NS + (j + 1))
                        nc.scalar.activation(log_term[j % 2][:, c0:], log_term[j % 2][:, c0:], ACT.Exp, scale=-1.0).then_inc(exp_ready, 1)
                        act.wait_ge(exp_ready, pair * NS + (j + 1))
                        nc.scalar.activation(log_term[j % 2][:, c0:], log_term[j % 2][:, c0:], ACT.Ln, bias=1.0).then_inc(log_ready, 1)
                    if 2 <= j < NS + 2:
                        i = j - 2
                        act.wait_ge(exponent_ready, pair * NS + (i + 1))
                        if i >= 2:
                            act.wait_ge(o_ready, pair * NS + (i - 1))
                        nc.scalar.activation(weights[i % 2][:, col0(i):], z_ps[i % 4][:, col0(i):], ACT.Exp).then_inc(weights_ready, 1)
                    if j - 3 in ends:
                        g = ends.index(j - 3)
                        s, h = groups[g]
                        act.wait_ge(o_ready, pair * NS + (ends[g] + 1))
                        if h == 0:
                            act.wait_ge(stored[s], pair * 16 + 16)
                        nc.scalar.activation(out_sb[s][:, h * HALF:(h + 1) * HALF], o_ps[g % 2][:, :], ACT.Copy).then_inc(o_copied, 1)
                        if h == 1:
                            act.wait_ge(o_copied, pair * 4 + (g + 1))
                            act.dma_start(out_dram[ds((pair * 2 + s) * 64, 64), :], out_sb[s][:, :]).then_inc(stored[s], 16)
            for s in range(2):
                act.wait_ge(stored[s], 16 * pairs + 16)



def load_phase(nc, name, pairs):
    with Phase(nc, name) as ph:
        loaded = ph.sem("loaded")
        block = ph.block()

        @block.sync
        def _(sp):
            for dst, src in pairs:
                sp.dma_start(dst, src).then_inc(loaded, 16)
            sp.wait_ge(loaded, 16 * len(pairs))


def short_conv_phase(nc, name, n_pairs, src, gate_before, gate_after, w, b, left, out):
    n_chunks = 2 * n_pairs
    with Phase(nc, name) as ph:
        taps, bias = ph.sb("taps", [P, n_chunks, 3]), ph.sb("bias", [P, n_chunks])
        z = [ph.sb(f"z{s}", [P, T + 2]) for s in range(2)]
        before = [ph.sb(f"before{s}", [P, T]) for s in range(2)]
        after = [ph.sb(f"after{s}", [P, T]) for s in range(2)]
        acc = [ph.sb(f"acc{s}", [P, T]) for s in range(2)]
        coef_loaded, padded = ph.sem("coef_loaded"), ph.sem("padded")
        loaded, used = [ph.sem(f"loaded{s}") for s in range(2)], [ph.sem(f"used{s}") for s in range(2)]
        stored, done = [ph.sem(f"stored{s}") for s in range(2)], ph.sem("done")
        block = ph.block()
        n_in = 1 + (gate_before is not None) + (gate_after is not None)
        n_ops = 3 + (gate_before is not None) + (gate_after is not None)

        @block.sync
        def _(sp):
            for i in range(3):
                sp.dma_start(taps[:, :, i], w[i].rearrange("(c p) -> p c", p=P),
                             allow_slow_non_contiguous=True).then_inc(coef_loaded, 16)
            load_columns(sp, bias[:, :], b, coef_loaded)

            def load(i, s):
                sp.dma_start(z[s][:, left:left + T], src(i * 2 + s)).then_inc(loaded[s], 16)
                if gate_before is not None:
                    sp.dma_start(before[s][:, :], gate_before(i * 2 + s)).then_inc(loaded[s], 16)
                if gate_after is not None:
                    sp.dma_start(after[s][:, :], gate_after(i * 2 + s)).then_inc(loaded[s], 16)

            for s in range(2):
                load(0, s)
            if n_pairs > 1:
                with sp.Fori(1, n_pairs) as i:
                    for s in range(2):
                        sp.wait_ge(used[s], i)
                        load(i, s)

        @block.vector
        def _(dve):
            for s in range(2):
                if left:
                    nc.vector.memset(z[s][:, 0:left], 0.0).then_inc(padded, 1)
                if left < 2:
                    nc.vector.memset(z[s][:, left + T:], 0.0).then_inc(padded, 1)
            dve.wait_ge(padded, 2 * ((left > 0) + (left < 2)))
            dve.wait_ge(coef_loaded, 16 * 4)
            for s in range(2):
                dve.sem_inc(stored[s], 16)
            with dve.Fori(0, n_pairs) as i:
                for s in range(2):
                    op = 0

                    def link(ins):
                        nonlocal op
                        op += 1
                        ins.then_inc(done, 1)
                        dve.wait_ge(done, i * (2 * n_ops) + (s * n_ops + op))

                    dve.wait_ge(loaded[s], i * (16 * n_in) + 16 * n_in)
                    if gate_before is not None:
                        link(nc.vector.tensor_tensor(z[s][:, left:left + T], z[s][:, left:left + T], before[s][:, :], ALU.mult))
                    dve.wait_ge(stored[s], i * 16 + 16)
                    tap = lambda n: taps[:, ds(i * 2 + s, 1), n]
                    link(nc.vector.tensor_scalar(acc[s][:, :], z[s][:, 0:T], tap(0), bias[:, ds(i * 2 + s, 1)],
                                                 ALU.mult, ALU.add))
                    for n in (1, 2):
                        link(nc.vector.scalar_tensor_tensor(out=acc[s][:, :], in0=z[s][:, n:n + T], scalar=tap(n),
                                                            in1=acc[s][:, :], op0=ALU.mult, op1=ALU.add))
                    if gate_after is not None:
                        link(nc.vector.tensor_tensor(acc[s][:, :], acc[s][:, :], after[s][:, :], ALU.mult))
                    dve.sem_inc(used[s], 1)

        @block.scalar
        def _(act):
            with act.Fori(0, n_pairs) as i:
                for s in range(2):
                    act.wait_ge(used[s], i + 1)
                    act.dma_start(out(i * 2 + s), acc[s][:, :]).then_inc(stored[s], 16)
            for s in range(2):
                act.wait_ge(stored[s], 16 * n_pairs + 16)


def gate_phase(nc, name, y, gate_rows, n_pairs=KD // 2):
    with Phase(nc, name) as ph:
        gate = [ph.sb(f"gate{s}", [P, T]) for s in range(2)]
        sig = [ph.sb(f"sig{s}", [P, T]) for s in range(2)]
        loaded, sig_ready = [ph.sem(f"loaded{s}") for s in range(2)], [ph.sem(f"sig_ready{s}") for s in range(2)]
        silu, used = ph.sem("silu"), [ph.sem(f"used{s}") for s in range(2)]
        block = ph.block()

        @block.sync
        def _(sp):
            for s in range(2):
                sp.dma_start(gate[s][:, :], gate_rows(s)).then_inc(loaded[s], 16)
            with sp.Fori(1, n_pairs) as i:
                for s in range(2):
                    sp.wait_ge(used[s], i)
                    sp.dma_start(gate[s][:, :], gate_rows(i * 2 + s)).then_inc(loaded[s], 16)

        @block.scalar
        def _(act):
            with act.Fori(0, n_pairs) as i:
                for s in range(2):
                    act.wait_ge(loaded[s], i * 16 + 16)
                    nc.scalar.activation(sig[s][:, :], gate[s][:, :], ACT.Sigmoid).then_inc(sig_ready[s], 1)

        @block.vector
        def _(dve):
            with dve.Fori(0, n_pairs) as i:
                for s in range(2):
                    dve.wait_ge(sig_ready[s], i + 1)
                    nc.vector.tensor_tensor(gate[s][:, :], gate[s][:, :], sig[s][:, :], ALU.mult).then_inc(silu, 1)
                for s in range(2):
                    rows = y[:, ds(i * 2 + s, 1), :]
                    dve.wait_ge(silu, i * 2 + (s + 1))
                    nc.vector.tensor_tensor(rows, rows, gate[s][:, :].rearrange("p (o t) -> p o t", o=1),
                                            ALU.mult).then_inc(used[s], 1)


def rope_phase(nc, name, rot, src, chunks, cos, sin, dst_rows):
    steps = [(n, c, h) for n, c in enumerate(chunks) for h in range(2)]
    with Phase(nc, name) as ph:
        moved = [ph.ps(f"moved{b}", [P, HALF]) for b in range(2)]
        sin_part = [ph.sb(f"sin_part{b}", [P, HALF]) for b in range(2)]
        cos_part = [ph.sb(f"cos_part{b}", [P, HALF]) for b in range(2)]
        out = [ph.sb(f"out{n}", [P, T]) for n in range(len(chunks))]
        moved_ready, parts_ready, out_ready, stored = ph.sem("moved_ready"), ph.sem("parts_ready"), ph.sem("out_ready"), ph.sem("stored")
        block = ph.block()

        @block.tensor
        def _(pe):
            for j, (n, c, h) in enumerate(steps):
                if j >= 2:
                    pe.wait_ge(parts_ready, 2 * (j - 1))
                nc.tensor.matmul(moved[j % 2][:, :], rot[:, :], src[:, c, h * HALF:(h + 1) * HALF], start=True,
                                 stop=True).then_inc(moved_ready, 1)

        @block.vector
        def _(dve):
            for j, (n, c, h) in enumerate(steps):
                t = slice(h * HALF, (h + 1) * HALF)
                if j >= 2:
                    dve.wait_ge(out_ready, j - 1)
                nc.vector.tensor_tensor(cos_part[j % 2][:, :], src[:, c, t], cos[:, t], ALU.mult).then_inc(parts_ready, 1)
                dve.wait_ge(moved_ready, j + 1)
                nc.vector.tensor_tensor(sin_part[j % 2][:, :], moved[j % 2][:, :], sin[:, t], ALU.mult).then_inc(parts_ready, 1)
                dve.wait_ge(parts_ready, 2 * (j + 1))
                nc.vector.tensor_tensor(out[n][:, t], cos_part[j % 2][:, :], sin_part[j % 2][:, :], ALU.add).then_inc(out_ready, 1)

        @block.sync
        def _(sp):
            for n in range(len(chunks)):
                sp.wait_ge(out_ready, 2 * n + 2)
                rows = dst_rows[n]
                sp.dma_start(rows, out[n][0:rows.shape[0], :]).then_inc(stored, 16)
            sp.wait_ge(stored, 16 * len(chunks))


def mod_phase(nc, name, ident, c_rows, w_mod, b_mod, cols):
    N = w_mod.shape[1]
    n_pairs = N // HALF // 2
    w_view = w_mod.rearrange("(c p) n -> p c n", p=P)
    with Phase(nc, name) as ph:
        cond, sig, silu = ph.sb("cond", [P, KD, 2]), ph.sb("sig", [P, KD, 2]), ph.sb("silu", [P, KD, 2])
        w_sb = [ph.sb(f"w{s}", [P, KD, HALF]) for s in range(2)]
        bias = [ph.sb(f"bias{s}", [2, HALF]) for s in range(2)]
        rows = [ph.sb(f"rows{s}", [2, HALF]) for s in range(2)]
        acc = [ph.ps(f"acc{s}", [2, HALF]) for s in range(2)]
        turned = [ph.ps(f"turned{s}", [P, 4, 2]) for s in range(2)]
        cond_loaded, sig_ready, silu_ready = ph.sem("cond_loaded"), ph.sem("sig_ready"), ph.sem("silu_ready")
        loaded, acc_ready = [ph.sem(f"loaded{s}") for s in range(2)], [ph.sem(f"acc_ready{s}") for s in range(2)]
        rows_ready, turned_ready = [ph.sem(f"rows_ready{s}") for s in range(2)], [ph.sem(f"turned_ready{s}") for s in range(2)]
        cols_ready = [ph.sem(f"cols_ready{s}") for s in range(2)]
        block = ph.block()

        @block.sync
        def _(sp):
            for r in range(2):
                sp.dma_start(cond[:, :, r], c_rows[r].rearrange("(c p) -> p c", p=P),
                             allow_slow_non_contiguous=True).then_inc(cond_loaded, 16)

            def load(i, s):
                sp.dma_start(w_sb[s][:, :, :], w_view[:, :, ds((i * 2 + s) * HALF, HALF)]).then_inc(loaded[s], 16)
                for r in range(2):
                    sp.dma_start(bias[s][r:r + 1, :], b_mod[0:1, ds((i * 2 + s) * HALF, HALF)]).then_inc(loaded[s], 16)

            for s in range(2):
                load(0, s)
            with sp.Fori(1, n_pairs) as i:
                for s in range(2):
                    sp.wait_ge(rows_ready[s], i)
                    load(i, s)

        @block.scalar
        def _(act):
            act.wait_ge(cond_loaded, 32)
            nc.scalar.activation(sig[:, :, :], cond[:, :, :], ACT.Sigmoid).then_inc(sig_ready, 1)

        @block.tensor
        def _(pe):
            pe.wait_ge(silu_ready, 1)
            with pe.Fori(0, n_pairs) as i:
                for s in range(2):
                    pe.wait_ge(loaded[s], i * 48 + 48)
                    pe.wait_ge(cols_ready[s], i + 1)
                    for c in range(KD):
                        mm = nc.tensor.matmul(acc[s][:, :], silu[:, c, :], w_sb[s][:, c, :], start=(c == 0), stop=(c == KD - 1))
                    mm.then_inc(acc_ready[s], 1)
                for s in range(2):
                    pe.wait_ge(silu_ready, 1)
                    pe.wait_ge(rows_ready[s], i + 1)
                    for b in range(4):
                        tr = nc.tensor.matmul(turned[s][:, b, :], rows[s][:, b * P:(b + 1) * P], ident[0:2, 0:2],
                                              start=True, stop=True)
                    tr.then_inc(turned_ready[s], 1)

        @block.vector
        def _(dve):
            dve.wait_ge(sig_ready, 1)
            nc.vector.tensor_tensor(silu[:, :, :], sig[:, :, :], cond[:, :, :], ALU.mult).then_inc(silu_ready, 1)
            for s in range(2):
                dve.sem_inc(cols_ready[s], 1)
            with dve.Fori(0, n_pairs) as i:
                for s in range(2):
                    dve.wait_ge(acc_ready[s], i + 1)
                    nc.vector.tensor_tensor(rows[s][:, :], acc[s][:, :], bias[s][:, :], ALU.add).then_inc(rows_ready[s], 1)
                for s in range(2):
                    dve.wait_ge(turned_ready[s], i + 1)
                    nc.vector.tensor_copy(cols[:, ds((i * 2 + s) * 4, 4), :], turned[s][:, :, :]).then_inc(cols_ready[s], 1)


ROUND = 1.5 * 2.0 ** 23
TWO_PI = 2 * np.pi


def two_pi_parts():
    left, parts = TWO_PI, []
    for _ in range(2):
        step = 2.0 ** (np.floor(np.log2(left)) - 10)
        parts.append(float(np.floor(left / step) * step))
        left -= parts[-1]
    return parts + [float(left)]


def reduce_angle(nc, eng, done, count, x, turns, shift):
    def link(ins):
        nonlocal count
        count += 1
        ins.then_inc(done, 1)
        eng.wait_ge(done, count)

    link(nc.vector.tensor_scalar(turns, x, 1 / TWO_PI, shift / TWO_PI, ALU.mult, ALU.add))
    link(nc.vector.tensor_scalar(turns, turns, ROUND, -ROUND, ALU.add, ALU.add))
    for part in two_pi_parts():
        link(nc.vector.scalar_tensor_tensor(out=x, in0=turns, scalar=-part, in1=x, op0=ALU.mult, op1=ALU.add))
    link(nc.vector.tensor_scalar(x, x, shift, 3.1415925, ALU.add, ALU.min))
    link(nc.vector.tensor_scalar(x, x, -3.1415925, None, ALU.max))
    return count


def filter_phase(nc, name, ones, featsT, w1, b1, w2, b2, w3, freq, decay, decay_back, even, odd, inv_norm):
    F, E = w1.shape[1], w1.shape[0]
    NT = T // P
    with Phase(nc, name) as ph:
        feats, w1_sb, w2_sb = ph.sb("feats", [E, T]), ph.sb("w1", [E, F]), ph.sb("w2", [F, F])
        w3_sb = ph.sb("w3", [F, 2 * HALF])
        consts = ph.sb("consts", [F, 3])
        hidden = [ph.sb(f"hidden{n}", [F, T]) for n in range(2)]
        turns = ph.sb("turns", [F, T])
        decays = [[ph.sb(f"decay{s}{d}", [P, HALF]) for d in range(2)] for s in range(2)]
        filt = [[ph.sb(f"filt{s}{d}", [P, HALF]) for d in range(2)] for s in range(2)]
        size = [[ph.sb(f"size{s}{d}", [P, HALF]) for d in range(2)] for s in range(2)]
        norm = ph.ps("norm", [P, HALF])
        pre = [ph.ps(f"pre{h}", [F, HALF]) for h in range(2)]
        taps = [[ph.ps(f"taps{s}{d}", [P, HALF]) for d in range(2)] for s in range(2)]
        loaded, pre_ready, done, hidden_ready = ph.sem("loaded"), ph.sem("pre_ready"), ph.sem("done"), ph.sem("hidden_ready")
        decay_loaded, taps_ready = [ph.sem(f"decay_loaded{s}") for s in range(2)], ph.sem("taps_ready")
        filt_ready, size_ready, summed, pair_ready = ph.sem("filt_ready"), ph.sem("size_ready"), ph.sem("summed"), ph.sem("pair_ready")
        block = ph.block()

        @block.sync
        def _(sp):
            for dst, src in ((feats[:, :], featsT), (w1_sb[:, :], w1), (w2_sb[:, :], w2), (w3_sb[:, :], w3)):
                sp.dma_start(dst, src).then_inc(loaded, 16)
            for n, v in enumerate((b1, b2, freq)):
                sp.dma_start(consts[:, n:n + 1], v.rearrange("(p o) -> p o", o=1)).then_inc(loaded, 16)
            for i in range(NT):
                if i >= 2:
                    sp.wait_ge(filt_ready, 2 * (i - 1))
                for d, src in enumerate((decay, decay_back)):
                    sp.dma_start(decays[i % 2][d][:, :], src[i * P:(i + 1) * P, :]).then_inc(decay_loaded[i % 2], 16)

        @block.tensor
        def _(pe):
            pe.wait_ge(loaded, 16 * 7)
            for layer, (w_sb, x) in enumerate(((w1_sb, feats), (w2_sb, hidden[0]))):
                if layer:
                    pe.wait_ge(hidden_ready, layer)
                for h in range(2):
                    nc.tensor.matmul(pre[h][:, :], w_sb[:, :], x[:, h * HALF:(h + 1) * HALF], start=True,
                                     stop=True).then_inc(pre_ready, 1)
            pe.wait_ge(hidden_ready, 2)

            def sizes(i):
                for d in range(2):
                    pe.wait_ge(size_ready, 2 * i + d + 1)
                    nc.tensor.matmul(norm[:, :], ones[:, :], size[i % 2][d][:, :], start=(i == 0 and d == 0),
                                     stop=(i == NT - 1 and d == 1)).then_inc(summed, 1)

            for i in range(NT):
                if i >= 2:
                    pe.wait_ge(filt_ready, 2 * (i - 1))
                for d in range(2):
                    nc.tensor.matmul(taps[i % 2][d][:, :], hidden[1][:, i * P:(i + 1) * P], w3_sb[:, d * HALF:(d + 1) * HALF],
                                     start=True, stop=True).then_inc(taps_ready, 1)
                if i >= 1:
                    sizes(i - 1)
            sizes(NT - 1)

        @block.vector
        def _(dve):
            dve.wait_ge(loaded, 16 * 7)
            count = 0
            for layer in range(2):
                for h in range(2):
                    dve.wait_ge(pre_ready, 2 * layer + h + 1)
                    nc.vector.tensor_scalar(hidden[layer][:, h * HALF:(h + 1) * HALF], pre[h][:, :], consts[:, layer:layer + 1],
                                            consts[:, 2:3], ALU.add, ALU.mult).then_inc(done, 1)
                count += 2
                dve.wait_ge(done, count)
                count = reduce_angle(nc, dve, done, count, hidden[layer][:, :], turns[:, :], 0.0)
            for i in range(NT):
                dve.wait_ge(decay_loaded[i % 2], 32 * (i // 2 + 1))
                if i >= 2:
                    dve.wait_ge(size_ready, 2 * (i - 1))
                for d in range(2):
                    dve.wait_ge(taps_ready, 2 * i + d + 1)
                    nc.vector.tensor_tensor(filt[i % 2][d][:, :], taps[i % 2][d][:, :], decays[i % 2][d][:, :],
                                            ALU.mult).then_inc(filt_ready, 1)
                dve.wait_ge(filt_ready, 2 * i + 2)
                nc.vector.tensor_tensor(even[:, i, :], filt[i % 2][0][:, :], filt[i % 2][1][:, :], ALU.add).then_inc(pair_ready, 1)
                nc.vector.tensor_tensor(odd[:, i, :], filt[i % 2][0][:, :], filt[i % 2][1][:, :], ALU.subtract).then_inc(pair_ready, 1)
                dve.wait_ge(pair_ready, 2 * i + 2)
            dve.wait_ge(summed, 2 * NT)
            nc.vector.reciprocal(inv_norm[:, :], norm[:, :]).then_inc(pair_ready, 1)

        @block.scalar
        def _(act):
            steps = 7
            for layer in range(2):
                act.wait_ge(done, (layer + 1) * (2 + steps))
                nc.scalar.activation(hidden[layer][:, :], hidden[layer][:, :], ACT.Sin).then_inc(hidden_ready, 1)
            for i in range(NT):
                for d in range(2):
                    act.wait_ge(filt_ready, 2 * i + d + 1)
                    if i >= 2:
                        act.wait_ge(summed, 2 * (i - 2) + d + 1)
                    nc.scalar.activation(size[i % 2][d][:, :], filt[i % 2][d][:, :], ACT.Abs).then_inc(size_ready, 1)


def spectrum_phase(nc, name, z_dram, h_dram, col0, inv_norm, y_dram):
    C = z_dram.shape[1]
    K = T // P
    with Phase(nc, name) as ph:
        z = [ph.sb(f"z{d}", [P, K, C]) for d in range(2)]
        f = [ph.sb(f"f{d}", [P, K, C]) for d in range(2)]
        prod = [ph.sb(f"prod{d}", [P, K, C]) for d in range(2)]
        y = [ph.sb(f"y{d}", [P, K, C]) for d in range(2)]
        loaded, scaled, prods, ready, stored = ph.sem("loaded"), ph.sem("scaled"), ph.sem("prods"), ph.sem("ready"), ph.sem("stored")
        block = ph.block()

        @block.sync
        def _(sp):
            for d in range(2):
                rows = slice(d * T, (d + 1) * T)
                sp.dma_start(f[d][:, :, :], h_dram[rows, col0:col0 + C].rearrange("(c p) n -> p c n", p=P)).then_inc(loaded, 16)
                sp.dma_start(z[d][:, :, :], z_dram[rows, :].rearrange("(c p) n -> p c n", p=P)).then_inc(loaded, 16)
            for d in range(2):
                sp.wait_ge(ready, d + 1)
                sp.dma_start(y_dram[d * T:(d + 1) * T, :].rearrange("(c p) n -> p c n", p=P), y[d][:, :, :]).then_inc(stored, 16)
            sp.wait_ge(stored, 32)

        @block.vector
        def _(dve):
            tt = nc.vector.tensor_tensor
            dve.wait_ge(loaded, 64)
            for d in range(2):
                for c in range(K):
                    tt(f[d][:, c, :], f[d][:, c, :], inv_norm[:, col0:col0 + C], ALU.mult).then_inc(scaled, 1)
            dve.wait_ge(scaled, 2 * K)
            tt(prod[0][:, :, :], z[0][:, :, :], f[0][:, :, :], ALU.mult).then_inc(prods, 1)
            tt(prod[1][:, :, :], z[1][:, :, :], f[1][:, :, :], ALU.mult).then_inc(prods, 1)
            dve.wait_ge(prods, 2)
            tt(y[0][:, :, :], prod[0][:, :, :], prod[1][:, :, :], ALU.subtract).then_inc(ready, 1)
            dve.wait_ge(ready, 1)
            tt(prod[0][:, :, :], z[0][:, :, :], f[1][:, :, :], ALU.mult).then_inc(prods, 1)
            tt(prod[1][:, :, :], z[1][:, :, :], f[0][:, :, :], ALU.mult).then_inc(prods, 1)
            dve.wait_ge(prods, 4)
            tt(y[1][:, :, :], prod[0][:, :, :], prod[1][:, :, :], ALU.add).then_inc(ready, 1)


def skip_gate_phase(nc, name, y_rows, z_rows, g_rows, d_vec, out_rows, chunks=2):
    with Phase(nc, name) as ph:
        y, z, g = ph.sb("y", [P, chunks, T]), ph.sb("z", [P, chunks, T]), ph.sb("g", [P, chunks, T])
        dcol = ph.sb("dcol", [P, chunks])
        loaded, summed, ready, stored = ph.sem("loaded"), ph.sem("summed"), ph.sem("ready"), ph.sem("stored")
        block = ph.block()

        @block.sync
        def _(sp):
            for dst, src in ((y, y_rows), (z, z_rows), (g, g_rows)):
                sp.dma_start(dst[:, :, :], src.rearrange("(c p) t -> p c t", p=P)).then_inc(loaded, 16)
            load_columns(sp, dcol[:, :], d_vec, loaded)
            sp.wait_ge(ready, chunks)
            sp.dma_start(out_rows.rearrange("(c p) t -> p c t", p=P), y[:, :, :]).then_inc(stored, 16)
            sp.wait_ge(stored, 16)

        @block.vector
        def _(dve):
            dve.wait_ge(loaded, 64)
            for c in range(chunks):
                nc.vector.scalar_tensor_tensor(out=y[:, c, :], in0=z[:, c, :], scalar=dcol[:, c:c + 1], in1=y[:, c, :],
                                               op0=ALU.mult, op1=ALU.add).then_inc(summed, 1)
            for c in range(chunks):
                dve.wait_ge(summed, c + 1)
                nc.vector.tensor_tensor(y[:, c, :], y[:, c, :], g[:, c, :], ALU.mult).then_inc(ready, 1)


def merge_phase(nc, name, branches, w_dram, gates, dst):
    KC = D // P
    spans, at = [], 0
    for rows in branches:
        spans.append((at, at + rows.shape[0] // P))
        at = spans[-1][1]
    NBR = len(branches)
    w_view = w_dram.rearrange("(c p) n -> p c n", p=P)
    n_pairs = KC // 2
    with Phase(nc, name) as ph:
        acts = ph.sb("acts", [P, KC, T])
        w_sb = [ph.sb(f"w{s}", [P, KC, P]) for s in range(2)]
        gate = [ph.sb(f"gate{s}", [P, NBR, T]) for s in range(2)]
        acc = [[ph.ps(f"acc{b}{h}", [P, HALF]) for h in range(2)] for b in range(NBR)]
        prod = [ph.sb(f"prod{b}", [P, T]) for b in range(NBR)]
        acts_loaded, loaded = ph.sem("acts_loaded"), [ph.sem(f"loaded{s}") for s in range(2)]
        gate_ready = [ph.sem(f"gate_ready{s}") for s in range(2)]
        acc_ready, prods, summed, tile_done = ph.sem("acc_ready"), ph.sem("prods"), ph.sem("summed"), ph.sem("tile_done")
        block = ph.block()

        @block.sync
        def _(sp):
            for (c0, c1), rows in zip(spans, branches):
                sp.dma_start(acts[:, c0:c1, :], rows.rearrange("(c p) t -> p c t", p=P)).then_inc(acts_loaded, 16)

            def load(i, s):
                sp.dma_start(w_sb[s][:, :, :], w_view[:, :, ds((i * 2 + s) * P, P)]).then_inc(loaded[s], 16)
                for b in range(NBR):
                    sp.dma_start(gate[s][:, b, :], gates(b, i * 2 + s)).then_inc(loaded[s], 16)

            for s in range(2):
                load(0, s)
            with sp.Fori(1, n_pairs) as i:
                for s in range(2):
                    sp.wait_ge(tile_done, i * 2 + (s - 1))
                    load(i, s)

        @block.scalar
        def _(act):
            with act.Fori(0, n_pairs) as i:
                for s in range(2):
                    act.wait_ge(loaded[s], i * (16 * (NBR + 1)) + 16 * (NBR + 1))
                    nc.scalar.activation(gate[s][:, :, :], gate[s][:, :, :], ACT.Sigmoid).then_inc(gate_ready[s], 1)

        @block.tensor
        def _(pe):
            pe.wait_ge(acts_loaded, 16 * NBR)
            with pe.Fori(0, n_pairs) as i:
                for s in range(2):
                    pe.wait_ge(loaded[s], i * (16 * (NBR + 1)) + 16 * (NBR + 1))
                    for b, (c0, c1) in enumerate(spans):
                        for h in range(2):
                            pe.wait_ge(prods, (i * 2 + s) * (2 * NBR) + (2 * b + h + 1))
                            for c in range(c0, c1):
                                mm = nc.tensor.matmul(acc[b][h][:, :], w_sb[s][:, c, :], acts[:, c, h * HALF:(h + 1) * HALF],
                                                      start=(c == c0), stop=(c == c1 - 1))
                            mm.then_inc(acc_ready, 1)

        @block.vector
        def _(dve):
            dve.sem_inc(prods, 2 * NBR)
            with dve.Fori(0, n_pairs) as i:
                for s in range(2):
                    for b in range(NBR):
                        for h in range(2):
                            t = slice(h * HALF, (h + 1) * HALF)
                            dve.wait_ge(acc_ready, (i * 2 + s) * (2 * NBR) + (2 * b + h + 1))
                            if b == 0 and h == 0:
                                dve.wait_ge(gate_ready[s], i + 1)
                            nc.vector.tensor_tensor(prod[b][:, t], acc[b][h][:, :], gate[s][:, b, t], ALU.mult).then_inc(prods, 1)
                    rows = dst[:, ds(i * 2 + s, 1), :]
                    flat = [prod[b][:, :].rearrange("p (o t) -> p o t", o=1) for b in range(NBR)]
                    dve.wait_ge(prods, (i * 2 + s) * (2 * NBR) + 4 * NBR)
                    nc.vector.tensor_tensor(rows, flat[0], flat[1], ALU.add).then_inc(summed, 1)
                    dve.wait_ge(summed, i * 2 + (s + 1))
                    nc.vector.tensor_tensor(rows, rows, flat[2], ALU.add).then_inc(tile_done, 1)
                    dve.wait_ge(tile_done, i * 2 + (s + 1))


N_EXPERTS, FF = 16, 2 * D
CAP = 2 * T // N_EXPERTS


def route_phase(nc, name, ident, iota_row, iota_col, hT, w_router, h_dram, token_of_slot, weight_of_slot):
    NT, E = T // P, N_EXPERTS
    with Phase(nc, name) as ph:
        w_sb = ph.sb("w", [P, KD, E])
        top, total, inv = ph.sb("top", [P, NT]), ph.sb("total", [P, NT]), ph.sb("inv", [P, NT])
        affT, work, mask = ph.sb("affT", [E, T]), ph.sb("work", [E, T]), ph.sb("mask", [E, T])
        ones, count, slot = ph.sb("ones", [E, T]), ph.sb("count", [E, T]), ph.sb("slot", [E, T])
        best = ph.sb("best", [E, 8])
        logits = ph.ps("logits", [P, NT, E])
        aff_ps = [ph.ps(f"aff{h}", [E, HALF]) for h in range(2)]
        slot_ps = ph.ps("slot_ps", [P, NT, E])
        turned = [ph.ps(f"turned{b}", [P, 4, P]) for b in range(2)]
        w_loaded, logits_ready, done = ph.sem("w_loaded"), ph.sem("logits_ready"), ph.sem("done")
        exp_ready, aff_ready, affT_ready = ph.sem("exp_ready"), ph.sem("aff_ready"), ph.sem("affT_ready")
        slot_ready, slotT_ready, stored = ph.sem("slot_ready"), ph.sem("slotT_ready"), [ph.sem(f"stored{b}") for b in range(2)]
        aff = ph.sb("aff", [P, NT, E])
        h_rows = [ph.sb(f"h_rows{b}", [P, D]) for b in range(2)]
        slot_col = ph.sb("slot_col", [P, NT, E])
        facts = ph.sb("facts", [P, NT, E, 2])
        sel = [ph.sb(f"sel{t}", [P, E, P]) for t in range(NT)]
        picked = ph.ps("picked", [P, E, 2])
        facts_ready, sel_ready, picked_ready = ph.sem("facts_ready"), ph.sem("sel_ready"), ph.sem("picked_ready")
        turned_ready, turned_copied = ph.sem("turned_ready"), ph.sem("turned_copied")
        block = ph.block()

        @block.sync
        def _(sp):
            sp.dma_start(w_sb[:, :, :], w_router.rearrange("(c p) e -> p c e", p=P)).then_inc(w_loaded, 16)
            for t in range(NT):
                sp.wait_ge(turned_copied, 2 * t + 2)
                sp.dma_start(h_dram[t * P:(t + 1) * P, :], h_rows[t % 2][:, :]).then_inc(stored[t % 2], 16)
            for b in range(2):
                sp.wait_ge(stored[b], 16 * (NT // 2))

        @block.tensor
        def _(pe):
            pe.wait_ge(w_loaded, 16)
            for t in range(NT):
                for c in range(KD):
                    mm = nc.tensor.matmul(logits[:, t, :], hT[:, c, t * P:(t + 1) * P], w_sb[:, c, :], start=(c == 0),
                                          stop=(c == KD - 1))
            mm.then_inc(logits_ready, 1)
            for g in range(2 * NT):
                t, f0 = g // 2, 4 * (g % 2)
                if g >= 2:
                    pe.wait_ge(turned_copied, g - 1)
                for b in range(4):
                    tr = nc.tensor.transpose(turned[g % 2][:, b, :], hT[:, f0 + b, t * P:(t + 1) * P], ident[:, :])
                tr.then_inc(turned_ready, 1)
            pe.wait_ge(aff_ready, 1)
            for t in range(NT):
                tr = nc.tensor.transpose(aff_ps[t // 4][:, (t % 4) * P:(t % 4 + 1) * P], aff[:, t, :], ident[:, :])
            tr.then_inc(affT_ready, 1)
            pe.wait_ge(slot_ready, 1)
            for t in range(NT):
                mm = nc.tensor.matmul(slot_ps[:, t, :], slot[:, t * P:(t + 1) * P], ident[0:E, 0:E], start=True, stop=True)
            mm.then_inc(slotT_ready, 1)
            pe.wait_ge(sel_ready, NT)
            pe.wait_ge(facts_ready, 2)
            for e in range(E):
                for t in range(NT):
                    mm = nc.tensor.matmul(picked[:, e, :], sel[t][:, e, :], facts[:, t, e, :], start=(t == 0), stop=(t == NT - 1))
            mm.then_inc(picked_ready, 1)

        @block.scalar
        def _(act):
            act.wait_ge(done, 2)
            nc.scalar.activation(aff[:, :, :], aff[:, :, :], ACT.Exp).then_inc(exp_ready, 1)
            for g in range(2 * NT):
                act.wait_ge(turned_ready, g + 1)
                t, f0 = g // 2, 4 * (g % 2)
                if t >= 2:
                    act.wait_ge(stored[t % 2], 16 * (t // 2))
                nc.scalar.activation(h_rows[t % 2][:, f0 * P:(f0 + 4) * P].rearrange("p (b n) -> p b n", b=4), turned[g % 2][:, :, :],
                                     ACT.Copy).then_inc(turned_copied, 1)

        @block.vector
        def _(dve):
            n = 0

            def link(ins):
                nonlocal n
                n += 1
                ins.then_inc(done, 1)
                dve.wait_ge(done, n)

            def spread(x):
                return x[:, :].rearrange("p (t o) -> p t o", o=1).to_broadcast([P, NT, E])

            dve.wait_ge(logits_ready, 1)
            link(nc.vector.reduce_max(top[:, :], logits[:, :, :], AX.X))
            link(nc.vector.tensor_tensor(aff[:, :, :], logits[:, :, :], spread(top), ALU.subtract))
            dve.wait_ge(exp_ready, 1)
            link(nc.vector.reduce_sum(total[:, :], aff[:, :, :], AX.X))
            link(nc.vector.reciprocal(inv[:, :], total[:, :]))
            nc.vector.tensor_tensor(aff[:, :, :], aff[:, :, :], spread(inv), ALU.mult).then_inc(aff_ready, 1)
            dve.wait_ge(affT_ready, 1)
            for h in range(2):
                link(nc.vector.tensor_copy(work[:, h * HALF:(h + 1) * HALF], aff_ps[h][:, :]))
            for _ in range(CAP // 8):
                link(nc.vector.max(best[:, :], work[:, :]))
                link(nc.vector.match_replace(out=work[:, :], in_to_replace=best[:, :], in_values=work[:, :], imm_value=-1.0))
            link(nc.vector.memset(ones[:, :], 1.0))
            link(nc.vector.tensor_scalar(mask[:, :], work[:, :], 0.0, None, ALU.is_lt))
            link(nc.vector.tensor_tensor_scan(out=count[:, :], data0=ones[:, :], data1=mask[:, :], initial=0.0, op0=ALU.mult,
                                              op1=ALU.add))
            link(nc.vector.tensor_tensor(count[:, :], count[:, :], mask[:, :], ALU.mult))
            nc.vector.tensor_scalar(slot[:, :], count[:, :], -1.0, None, ALU.add).then_inc(slot_ready, 1)
            dve.wait_ge(slotT_ready, 1)
            link(nc.vector.tensor_copy(slot_col[:, :, :], slot_ps[:, :, :]))
            for t in range(NT):
                nc.vector.tensor_tensor(sel[t][:, :, :], iota_row.rearrange("p (o c) -> p o c", o=1).to_broadcast([P, E, P]),
                                        slot_col[:, t, :].rearrange("p (e o) -> p e o", o=1).to_broadcast([P, E, P]),
                                        ALU.is_equal).then_inc(sel_ready, 1)
            nc.vector.tensor_copy(facts[:, :, :, 0], aff[:, :, :]).then_inc(facts_ready, 1)
            for t in range(NT):
                ins = nc.vector.tensor_scalar(facts[:, t, :, 1], iota_col[:, 0:E], float(t * P), None, ALU.add)
            ins.then_inc(facts_ready, 1)
            dve.wait_ge(picked_ready, 1)
            nc.vector.tensor_copy(weight_of_slot[:, :], picked[:, :, 0]).then_inc(facts_ready, 1)
            nc.vector.tensor_copy(token_of_slot[:, :], picked[:, :, 1]).then_inc(facts_ready, 1)


def expert_phase(nc, name, ident, h_dram, token_of_slot, weight_of_slot, w_gate, w_up, w_down, sums_dram):
    E, NT = N_EXPERTS, T // P
    NF = FF // HALF
    CH, RING, HIS = 24, 4, 4
    GU = 4 * NF
    with Phase(nc, name) as ph:
        ring = [ph.sb(f"ring{r}", [P, 4, HALF]) for r in range(RING)]
        w_hi = [ph.sb(f"w_hi{r}", [P, 4, HALF], F32R) for r in range(HIS)]
        w_lo = [ph.sb(f"w_lo{r}", [P, 4, HALF], F32R) for r in range(HIS)]
        rows = ph.sb("rows", [P, D])
        xg_hi, xg_lo = ph.sb("xg_hi", [P, KD, P], F32R), ph.sb("xg_lo", [P, KD, P], F32R)
        sig = [ph.sb(f"sig{b}", [P, HALF]) for b in range(2)]
        act_sb = [ph.sb(f"act{b}", [P, HALF]) for b in range(2)]
        act_hi, act_lo = ph.sb("act_hi", [P, 4 * NF, P], F32R), ph.sb("act_lo", [P, 4 * NF, P], F32R)
        y_sb = ph.sb("y", [P, D])
        idx_in, idx_out = ph.sb("idx_in", [P, 1], U32), ph.sb("idx_out", [P, 1], U32)
        gate_ps = [ph.ps(f"gate{b}", [P, HALF]) for b in range(2)]
        up_ps = [ph.ps(f"up{b}", [P, HALF]) for b in range(2)]
        turned, x_turned = ph.ps("turned", [P, 4, P]), ph.ps("x_turned", [P, 4, P])
        y_ps = [ph.ps(f"y_ps{h}", [P, HALF]) for h in range(2)]
        loaded = [ph.sem(f"loaded{r}") for r in range(RING)]
        chunks_used, hi_ready = ph.sem("chunks_used"), ph.sem("hi_ready")
        lo_dve, lo_pool = ph.sem("lo_dve"), ph.sem("lo_pool")
        zero_ready, zeroed, moved = ph.sem("zero_ready"), ph.sem("zeroed"), ph.sem("moved")
        pool_step, idx_ready = ph.sem("pool_step"), ph.sem("idx_ready")
        x_turned_ready, xg_hi_ready, xg_ready = ph.sem("x_turned_ready"), ph.sem("xg_hi_ready"), ph.sem("xg_ready")
        sig_ready, prod_ready, act_ready, turned_ready = (ph.sem("sig_ready"), ph.sem("prod_ready"), ph.sem("act_ready"),
                                                          ph.sem("turned_ready"))
        act_hi_ready, actT_ready, y_free, y_ready = (ph.sem("act_hi_ready"), ph.sem("actT_ready"), ph.sem("y_free"),
                                                     ph.sem("y_ready"))
        block = ph.block()
        PER_SLOT = CH // RING

        def used(e, n):
            return e * CH + (RING + n)

        def experts(eng, body):
            with eng.Fori(0, E - 1) as e:
                body(e, False)
            body(E - 1, True)

        @block.sync
        def _(sp):
            sp.wait_ge(zero_ready, 1)
            for t in range(NT):
                sp.dma_start(sums_dram[t * P:(t + 1) * P, :], y_sb[:, :]).then_inc(zeroed, 16)
            with sp.Fori(0, E) as e:
                for n in range(CH):
                    for split in (lo_dve, lo_pool):
                        sp.wait_ge(split, e * CH + (n + 1))
                    dst = ring[n % RING][:, :, :]
                    if n < GU:
                        f, k0 = n // 4, (n % 2) * HALF
                        w = (w_gate, w_up)[n // 2 % 2]
                        src = w[ds(e, 1), k0:k0 + HALF, f * HALF:(f + 1) * HALF].rearrange("o (c p) n -> p (o c) n", p=P)
                    else:
                        r0 = (n - GU) * 2 * P
                        src = w_down[ds(e, 1), r0:r0 + 2 * P, :].rearrange("o (c p) n -> p (o c) n", p=P)
                        dst = dst.rearrange("p (c h) n -> p c (h n)", c=2)
                    sp.dma_start(dst, src).then_inc(loaded[n % RING], 16)

        @block.tensor
        def _(pe):
            def turn_rows(e, b):
                if b:
                    pe.wait_ge(xg_ready, e * 2 + 1)
                for j in range(4):
                    f = 4 * b + j
                    tr = nc.tensor.transpose(x_turned[:, j, :], rows[:, f * P:(f + 1) * P], ident[:, :])
                tr.then_inc(x_turned_ready, 1)

            def body(e, last):
                def chunk(n):
                    for split in (lo_dve, lo_pool):
                        pe.wait_ge(split, used(e, n + 1))
                    return w_hi[n % HIS], w_lo[n % HIS]

                def gate_up(f):
                    if f >= 2:
                        pe.wait_ge(act_ready, e * NF + (f - 1))
                    elif f == 0:
                        pe.wait_ge(xg_ready, e * 2 + 2)
                    for n in range(4 * f, 4 * f + 4):
                        hi, lo = chunk(n)
                        bank = (gate_ps, up_ps)[n // 2 % 2][f % 2]
                        for j in range(4):
                            c = 4 * (n % 2) + j
                            mm = split_products(nc, bank[:, :], xg_hi[:, c, :], xg_lo[:, c, :], hi[:, j, :],
                                                lo[:, j, :], c == 0, c == KD - 1)
                        mm.then_inc(chunks_used, 1)

                def turn(f):
                    pe.wait_ge(act_ready, e * NF + (f + 1))
                    if f >= 1:
                        pe.wait_ge(actT_ready, e * NF + f)
                    for b in range(4):
                        tr = nc.tensor.transpose(turned[:, b, :], act_sb[f % 2][:, b * P:(b + 1) * P], ident[:, :])
                    tr.then_inc(turned_ready, 1)

                def down(d):
                    hi, lo = chunk(GU + d)
                    pe.wait_ge(actT_ready, e * NF + (d // 2 + 1))
                    for j in range(2):
                        for h in range(2):
                            mm = split_products(nc, y_ps[h][:, :], act_hi[:, 2 * d + j, :], act_lo[:, 2 * d + j, :],
                                                hi[:, 2 * j + h, :], lo[:, 2 * j + h, :],
                                                d == 0 and j == 0, d == CH - GU - 1 and j == 1)
                    mm.then_inc(chunks_used, 1)

                gate_up(0)
                for f in range(1, NF):
                    gate_up(f)
                    turn(f - 1)
                pe.wait_ge(y_ready, e * 2 + 2)
                for d in range(CH - GU):
                    down(d)
                    if d == 1:
                        turn(NF - 1)
                        if not last:
                            pe.wait_ge(moved, e * 32 + 32)
                            turn_rows(e + 1, 0)
                    if d == 3 and not last:
                        turn_rows(e + 1, 1)

            pe.sem_inc(chunks_used, RING)
            pe.wait_ge(moved, 16)
            turn_rows(0, 0)
            turn_rows(0, 1)
            experts(pe, body)

        @block.scalar
        def _(act):
            def split(e, n):
                act.wait_ge(loaded[n % RING], e * (16 * PER_SLOT) + 16 * (n // RING + 1))
                act.wait_ge(chunks_used, used(e, n - HIS + 1))
                nc.scalar.activation(w_hi[n % HIS][:, :, :], ring[n % RING][:, :, :], ACT.Copy).then_inc(hi_ready, 1)

            def body(e, last):
                for f in range(NF):
                    for n in range(4 * f + 4, 4 * f + 6):
                        split(e, n)
                    act.wait_ge(chunks_used, used(e, 4 * f + 2))
                    if f >= 2:
                        act.wait_ge(act_ready, e * NF + (f - 1))
                    nc.scalar.activation(sig[f % 2][:, :], gate_ps[f % 2][:, :], ACT.Sigmoid).then_inc(sig_ready, 1)
                    for n in range(4 * f + 6, 4 * f + 8):
                        split(e, n)
                for n in range(GU + 4, CH):
                    split(e, n)
                if not last:
                    for n in range(4):
                        split(e + 1, n)
                act.wait_ge(y_free, e + 1)
                act.wait_ge(chunks_used, used(e, CH))
                for h in range(2):
                    nc.scalar.activation(y_sb[:, h * HALF:(h + 1) * HALF], y_ps[h][:, :], ACT.Copy,
                                         scale=weight_of_slot[:, ds(e, 1)]).then_inc(y_ready, 1)

            act.sem_inc(y_ready, 2)
            for n in range(4):
                split(0, n)
            experts(act, body)

        @block.vector
        def _(dve):
            def split(e, n):
                dve.wait_ge(hi_ready, e * CH + (n + 1))
                nc.vector.tensor_tensor(w_lo[n % HIS][:, 0:3, :], ring[n % RING][:, 0:3, :],
                                        w_hi[n % HIS][:, 0:3, :].bitcast(F32), ALU.subtract).then_inc(lo_dve, 1)

            def split_rows(e, b):
                at = slice(4 * b, 4 * b + 4)
                dve.wait_ge(x_turned_ready, e * 2 + (b + 1))
                split_hi(nc, xg_hi[:, at, :], x_turned[:, :, :]).then_inc(xg_hi_ready, 1)
                dve.wait_ge(xg_hi_ready, e * 2 + (b + 1))
                nc.vector.tensor_tensor(xg_lo[:, at, :], x_turned[:, :, :], xg_hi[:, at, :].bitcast(F32),
                                        ALU.subtract).then_inc(xg_ready, 1)

            def silu(e, f):
                dve.wait_ge(sig_ready, e * NF + (f + 1))
                if f >= 2:
                    dve.wait_ge(turned_ready, e * NF + (f - 1))
                nc.vector.tensor_tensor(act_sb[f % 2][:, :], gate_ps[f % 2][:, :], sig[f % 2][:, :], ALU.mult).then_inc(prod_ready, 1)
                dve.wait_ge(prod_ready, e * NF + (f + 1))
                dve.wait_ge(chunks_used, used(e, 4 * f + 4))
                nc.vector.tensor_tensor(act_sb[f % 2][:, :], up_ps[f % 2][:, :], act_sb[f % 2][:, :], ALU.mult).then_inc(act_ready, 1)

            def split_act(e, f):
                at = slice(4 * f, 4 * f + 4)
                dve.wait_ge(turned_ready, e * NF + (f + 1))
                split_hi(nc, act_hi[:, at, :], turned[:, :, :]).then_inc(act_hi_ready, 1)
                dve.wait_ge(act_hi_ready, e * NF + (f + 1))
                nc.vector.tensor_tensor(act_lo[:, at, :], turned[:, :, :], act_hi[:, at, :].bitcast(F32),
                                        ALU.subtract).then_inc(actT_ready, 1)

            def body(e, last):
                for f in range(NF):
                    for n in range(4 * f + 4, 4 * f + 8):
                        split(e, n)
                    silu(e, f)
                    if f >= 1:
                        split_act(e, f - 1)
                split(e, GU + 4)
                split(e, GU + 5)
                split_act(e, NF - 1)
                if not last:
                    split_rows(e + 1, 0)
                split(e, GU + 6)
                split(e, GU + 7)
                if not last:
                    split_rows(e + 1, 1)
                    for n in range(4):
                        split(e + 1, n)

            nc.vector.memset(y_sb[:, :], 0.0).then_inc(zero_ready, 1)
            dve.sem_inc(lo_dve, RING)
            for b in range(2):
                split_rows(0, b)
            for n in range(4):
                split(0, n)
            experts(dve, body)

        @block.gpsimd
        def _(pool):
            def split(e, n):
                pool.wait_ge(hi_ready, e * CH + (n + 1))
                nc.gpsimd.tensor_tensor(w_lo[n % HIS][:, 3, :], ring[n % RING][:, 3, :], w_hi[n % HIS][:, 3, :].bitcast(F32),
                                        ALU.subtract).then_inc(lo_pool, 1)

            def gather(e, idx_count):
                nc.gpsimd.tensor_copy(idx_in[:, :], token_of_slot[:, ds(e, 1)]).then_inc(idx_ready, 1)
                pool.wait_ge(idx_ready, idx_count)
                pool.sem_inc(pool_step, 1)
                nc.gpsimd.indirect_dma_start(rows[:, :], None, h_dram, bass.IndirectOffsetOnAxis(idx_in[:, 0:1], 0)).then_inc(moved, 16)

            def body(e, last):
                pool.wait_ge(moved, e * 32 + 16)
                pool.sem_inc(y_free, 1)
                if not last:
                    pool.wait_ge(x_turned_ready, e * 2 + 2)
                    pool.sem_inc(pool_step, 1)
                    gather(e + 1, e * 2 + 2)
                for n in range(4, CH):
                    split(e, n)
                if not last:
                    for n in range(4):
                        split(e + 1, n)
                pool.wait_ge(y_ready, e * 2 + 4)
                pool.sem_inc(pool_step, 1)
                pool.wait_ge(moved, e * 32 + (16 if last else 32))
                pool.sem_inc(pool_step, 1)
                nc.gpsimd.tensor_copy(idx_out[:, :], token_of_slot[:, ds(e, 1)]).then_inc(idx_ready, 1)
                pool.wait_ge(idx_ready, e * 2 + (2 if last else 3))
                pool.sem_inc(pool_step, 1)
                nc.gpsimd.indirect_dma_start(sums_dram, bass.IndirectOffsetOnAxis(idx_out[:, 0:1], 0), y_sb[:, :], None,
                                             compute_op=ALU.add).then_inc(moved, 16)

            pool.sem_inc(lo_pool, RING)
            gather(0, 1)
            for n in range(4):
                split(0, n)
            pool.wait_ge(zeroed, 16 * NT)
            experts(pool, body)
            pool.wait_ge(moved, 32 * E)


def add_turned_phase(nc, name, ident, src_dram, gain, x):
    NT = T // P
    with Phase(nc, name) as ph:
        rows = [ph.sb(f"rows{s}", [P, D]) for s in range(2)]
        turned = [[ph.ps(f"turned{s}{b}", [P, 4, P]) for b in range(2)] for s in range(2)]
        loaded = [ph.sem(f"loaded{s}") for s in range(2)]
        turned_ready, added = ph.sem("turned_ready"), ph.sem("added")
        block = ph.block()

        @block.sync
        def _(sp):
            for t in range(NT):
                if t >= 2:
                    sp.wait_ge(turned_ready, 2 * (t - 1))
                sp.dma_start(rows[t % 2][:, :], src_dram[t * P:(t + 1) * P, :]).then_inc(loaded[t % 2], 16)

        @block.tensor
        def _(pe):
            for t in range(NT):
                pe.wait_ge(loaded[t % 2], 16 * (t // 2 + 1))
                if t >= 2:
                    pe.wait_ge(added, KD * (t - 1))
                for b in range(2):
                    for j in range(4):
                        f = 4 * b + j
                        tr = nc.tensor.transpose(turned[t % 2][b][:, j, :], rows[t % 2][:, f * P:(f + 1) * P], ident[:, :])
                    tr.then_inc(turned_ready, 1)

        @block.vector
        def _(dve):
            for t in range(NT):
                for f in range(KD):
                    dve.wait_ge(turned_ready, 2 * t + f // 4 + 1)
                    out = x[:, f, t * P:(t + 1) * P]
                    nc.vector.scalar_tensor_tensor(out=out, in0=turned[t % 2][f // 4][:, f % 4, :], scalar=gain[:, f:f + 1],
                                                   in1=out, op0=ALU.mult, op1=ALU.add).then_inc(added, 1)


def angle_phase(nc, name, positions, freq_col, cos, sin):
    with Phase(nc, name) as ph:
        pos = ph.sb("pos", [P, T], I32)
        posf, turns, freq = ph.sb("posf", [P, T]), ph.sb("turns", [P, T]), ph.sb("freq", [P, 1])
        loaded, done, ready = ph.sem("loaded"), ph.sem("done"), ph.sem("ready")
        block = ph.block()

        @block.sync
        def _(sp):
            sp.dma_start(pos[:, :], positions.to_broadcast([P, T])).then_inc(loaded, 16)
            sp.dma_start(freq[:, :], freq_col).then_inc(loaded, 16)

        @block.vector
        def _(dve):
            dve.wait_ge(loaded, 32)
            nc.vector.tensor_copy(posf[:, :], pos[:, :]).then_inc(done, 1)
            dve.wait_ge(done, 1)
            for out in (sin, cos):
                nc.vector.tensor_scalar(out[:, :], posf[:, :], freq[:, 0:1], None, ALU.mult).then_inc(done, 1)
            dve.wait_ge(done, 3)
            count = 3
            for out, shift in ((sin, 0.0), (cos, np.pi / 2)):
                count = reduce_angle(nc, dve, done, count, out[:, :], turns[:, :], float(shift))

        @block.scalar
        def _(act):
            for n, out in enumerate((sin, cos)):
                act.wait_ge(done, 3 + 7 * (n + 1))
                nc.scalar.activation(out[:, :], out[:, :], ACT.Sin).then_inc(ready, 1)
            act.wait_ge(ready, 2)


def token_shift_phase(nc, name, n_chunks, src, mu, out):
    n_pairs, odd = n_chunks // 2, n_chunks % 2
    with Phase(nc, name) as ph:
        mix = ph.sb("mix", [P, n_chunks])
        p = [ph.sb(f"p{s}", [P, T + 1]) for s in range(2)]
        diff = [ph.sb(f"diff{s}", [P, T]) for s in range(2)]
        mix_loaded, padded = ph.sem("mix_loaded"), ph.sem("padded")
        loaded, diff_ready = [ph.sem(f"loaded{s}") for s in range(2)], [ph.sem(f"diff_ready{s}") for s in range(2)]
        ready, stored = [ph.sem(f"ready{s}") for s in range(2)], [ph.sem(f"stored{s}") for s in range(2)]
        block = ph.block()

        def turns(eng, body):
            with eng.Fori(0, n_pairs) as i:
                for s in range(2):
                    body(i, s)
            if odd:
                body(n_pairs, 0)

        @block.sync
        def _(sp):
            load_columns(sp, mix[:, :], mu, mix_loaded)

            def load(i, s):
                sp.wait_ge(ready[s], i + 1)
                sp.dma_start(p[s][:, 1:], src(i * 2 + s)).then_inc(loaded[s], 16)

            turns(sp, load)

        @block.vector
        def _(dve):
            for s in range(2):
                nc.vector.memset(p[s][:, 0:1], 0.0).then_inc(padded, 1)
                dve.sem_inc(ready[s], 1)
                dve.sem_inc(stored[s], 16)
            dve.wait_ge(padded, 2)
            dve.wait_ge(mix_loaded, 16)

            def body(i, s):
                dve.wait_ge(loaded[s], i * 16 + 16)
                dve.wait_ge(stored[s], i * 16 + 16)
                nc.vector.tensor_tensor(diff[s][:, :], p[s][:, 0:T], p[s][:, 1:], ALU.subtract).then_inc(diff_ready[s], 1)
                dve.wait_ge(diff_ready[s], i + 1)
                nc.vector.scalar_tensor_tensor(out=diff[s][:, :], in0=diff[s][:, :], scalar=mix[:, ds(i * 2 + s, 1)],
                                               in1=p[s][:, 1:], op0=ALU.mult, op1=ALU.add).then_inc(ready[s], 1)

            turns(dve, body)

        @block.scalar
        def _(act):
            def store(i, s):
                act.wait_ge(ready[s], i + 2)
                act.dma_start(out(i * 2 + s), diff[s][:, :]).then_inc(stored[s], 16)

            turns(act, store)
            for s in range(2):
                act.wait_ge(stored[s], 16 * (n_pairs + 1) + 16 * (odd and s == 0))


RW = 512
RC = RW // P
CHUNK = 64
NCH = T // CHUNK


def lora_phase(nc, name, x_rows, w_in_a, w_in_b, bias_a, bias_b, sig_a, sig_b):
    with Phase(nc, name) as ph:
        x = ph.sb("x", [P, T])
        w = [ph.sb(f"w{n}", [P, RW]) for n in range(2)]
        bias = [ph.sb(f"bias{n}", [P, RC]) for n in range(2)]
        acc = [ph.ps(f"acc{b}", [P, HALF]) for b in range(4)]
        zeroed, loaded, x_ready, acc_ready, out_ready = (ph.sem("zeroed"), ph.sem("loaded"), ph.sem("x_ready"), ph.sem("acc_ready"),
                                                         ph.sem("out_ready"))
        block = ph.block()
        steps = [(n, c, h) for n in range(2) for c in range(RC) for h in range(2)]

        @block.sync
        def _(sp):
            sp.dma_start(x[:, :], x_rows).then_inc(loaded, 16)
            for n, (src, b) in enumerate(((w_in_a, bias_a), (w_in_b, bias_b))):
                sp.dma_start(w[n][64 * n:64 * n + 64, :], src).then_inc(loaded, 16)
                load_columns(sp, bias[n][:, :], b, loaded)

        @block.vector
        def _(dve):
            for n in range(2):
                nc.vector.memset(w[n][64 - 64 * n:128 - 64 * n, :], 0.0).then_inc(zeroed, 1)

        @block.scalar
        def _(act):
            act.wait_ge(loaded, 16 * 5)
            nc.scalar.activation(x[0:64, :], x[0:64, :], ACT.Tanh).then_inc(x_ready, 1)
            for j, (n, c, h) in enumerate(steps):
                act.wait_ge(acc_ready, j + 1)
                nc.scalar.activation((sig_a, sig_b)[n][:, c, h * HALF:(h + 1) * HALF], acc[j % 4][:, :], ACT.Sigmoid,
                                     bias=bias[n][:, c:c + 1]).then_inc(out_ready, 1)

        @block.tensor
        def _(pe):
            pe.wait_ge(x_ready, 1)
            pe.wait_ge(zeroed, 2)
            for j, (n, c, h) in enumerate(steps):
                if j >= 4:
                    pe.wait_ge(out_ready, j - 3)
                nc.tensor.matmul(acc[j % 4][:, :], w[n][:, c * P:(c + 1) * P], x[:, h * HALF:(h + 1) * HALF], start=True,
                                 stop=True).then_inc(acc_ready, 1)


def scale_rows_phase(nc, name, rows, vec, dst):
    C = len(rows)
    with Phase(nc, name) as ph:
        col = ph.sb("col", [P, C])
        loaded, ready = ph.sem("loaded"), ph.sem("ready")
        block = ph.block()

        @block.sync
        def _(sp):
            load_columns(sp, col[:, :], vec, loaded)
            for c in range(C):
                sp.dma_start(dst[:, c, :], rows[c]).then_inc(loaded, 16)

        @block.vector
        def _(dve):
            dve.wait_ge(loaded, 16 * (C + 1))
            for c in range(C):
                nc.vector.tensor_scalar(dst[:, c, :], dst[:, c, :], col[:, c:c + 1], None, ALU.mult).then_inc(ready, 1)


def recurrence_inputs_phase(nc, name, block_ones, ps_rows, kk, decay_sig, rate, k_a, r_k, ends, bonus, out):
    with Phase(nc, name) as ph:
        r, k, v = ([ph.sb(f"{n}{s}", [P, T]) for s in range(2)] for n in "rkv")
        keep = ph.sb("keep", [P, T])
        cols = ph.sb("cols", [P, 2, RC])
        log_p, log_prev = ph.sb("log_p", [P, T]), ph.sb("log_prev", [P, T])
        p_now, p_inv, p_prev = ph.sb("p_now", [P, T]), ph.sb("p_inv", [P, T]), ph.sb("p_prev", [P, T])
        outs = [ph.sb(f"out{n}", [P, T]) for n in range(4)]
        kf = ph.sb("kf", [P, T])
        sums = [ph.ps(f"sums{h}", [P, HALF]) for h in range(2)]
        cols_loaded, done = ph.sem("cols_loaded"), ph.sem("done")
        loaded = [ph.sem(f"loaded{s}") for s in range(2)]
        logs_ready, exps_ready, rk_ready, sums_ready = ph.sem("logs_ready"), ph.sem("exps_ready"), ph.sem("rk_ready"), ph.sem("sums_ready")
        out_ready, chunk_done, stored = ph.sem("out_ready"), ph.sem("chunk_done"), ph.sem("stored")
        block = ph.block()

        @block.sync
        def _(sp):
            for n, vec in enumerate((k_a, r_k)):
                load_columns(sp, cols[:, n, :], vec, cols_loaded)
            for c in range(RC):
                if c >= 2:
                    sp.wait_ge(chunk_done, c - 1)
                for n, dst in enumerate((r, k, v)):
                    sp.dma_start(dst[c % 2][:, :], ps_rows(n * RC + c)).then_inc(loaded[c % 2], 16)

        @block.vector
        def _(dve):
            n_done = 0

            def link(ins):
                nonlocal n_done
                n_done += 1
                ins.then_inc(done, 1)
                dve.wait_ge(done, n_done)

            tt, stt, ts = nc.vector.tensor_tensor, nc.vector.scalar_tensor_tensor, nc.vector.tensor_scalar
            link(nc.vector.memset(keep[:, :], 1.0))
            link(nc.vector.memset(keep[:, :].rearrange("p (n t) -> p n t", t=CHUNK)[:, :, 0:1], 0.0))
            dve.wait_ge(cols_loaded, 32)
            for c in range(RC):
                s = c % 2
                if c:
                    dve.wait_ge(exps_ready, 3 * c)
                link(ts(decay_sig[:, c, :], decay_sig[:, c, :], -float(np.exp(-0.5)), None, ALU.mult))
                link(nc.vector.tensor_tensor_scan(out=log_p[:, :], data0=keep[:, :], data1=decay_sig[:, c, :], initial=0.0,
                                                  op0=ALU.mult, op1=ALU.add))
                tt(log_prev[:, :], log_p[:, :], decay_sig[:, c, :], ALU.subtract).then_inc(logs_ready, 1)
                dve.wait_ge(loaded[s], 48 * (c // 2 + 1))
                link(ts(kf[:, :], rate[:, c, :], 1.0, cols[:, 0, c:c + 1], ALU.subtract, ALU.mult))
                link(stt(out=kf[:, :], in0=kf[:, :], scalar=1.0, in1=k[s][:, :], op0=ALU.add, op1=ALU.mult))
                stt(out=k[s][:, :], in0=r[s][:, :], scalar=cols[:, 1, c:c + 1], in1=kf[:, :], op0=ALU.mult,
                    op1=ALU.mult).then_inc(rk_ready, 1)
                dve.wait_ge(exps_ready, 3 * c + 3)
                if c:
                    dve.wait_ge(stored, 64 * c)
                link(tt(outs[0][:, :], p_prev[:, :], kk[:, c, :], ALU.mult))
                link(tt(outs[1][:, :], rate[:, c, :], kk[:, c, :], ALU.mult))
                link(tt(outs[1][:, :], outs[1][:, :], p_inv[:, :], ALU.mult))
                link(tt(outs[2][:, :], kf[:, :], p_inv[:, :], ALU.mult))
                link(tt(outs[3][:, :], p_now[:, :], r[s][:, :], ALU.mult))
                link(nc.vector.tensor_copy(ends[:, c, :], p_now[:, :].rearrange("p (n t) -> p n t", t=CHUNK)[:, :, CHUNK - 1]))
                dve.sem_inc(out_ready, 1)
                for h in range(2):
                    dve.wait_ge(sums_ready, 2 * c + h + 1)
                    t = slice(h * HALF, (h + 1) * HALF)
                    link(tt(bonus[:, c, t], sums[h][:, :], v[s][:, t], ALU.mult))
                dve.sem_inc(chunk_done, 1)

        @block.scalar
        def _(act):
            for c in range(RC):
                act.wait_ge(logs_ready, c + 1)
                if c:
                    act.wait_ge(chunk_done, c)
                for dst, src, sign in ((p_now, log_p, 1.0), (p_inv, log_p, -1.0), (p_prev, log_prev, 1.0)):
                    nc.scalar.activation(dst[:, :], src[:, :], ACT.Exp, scale=sign).then_inc(exps_ready, 1)
                act.wait_ge(out_ready, c + 1)
                for n in range(4):
                    act.dma_start(out[n][c * P:(c + 1) * P, :], outs[n][:, :]).then_inc(stored, 16)
            act.wait_ge(stored, 64 * RC)

        @block.tensor
        def _(pe):
            for c in range(RC):
                pe.wait_ge(rk_ready, c + 1)
                if c:
                    pe.wait_ge(chunk_done, c)
                for h in range(2):
                    nc.tensor.matmul(sums[h][:, :], block_ones[:, :], k[c % 2][:, h * HALF:(h + 1) * HALF], start=True,
                                     stop=True).then_inc(sums_ready, 1)


LEVELS = 6


def recurrence_masks():
    i = np.arange(P)
    same = (i[:, None] // CHUNK) == (i[None, :] // CHUNK)
    row, col = i[:, None] % CHUNK, i[None, :] % CHUNK
    masks = [same & (row < col), same & (row <= col)]

    def level(b):
        return same & (row // (2 * b) == col // (2 * b)) & (row % (2 * b) >= b) & (col % (2 * b) < b)

    first = level(1)
    out = [m.astype(np.float32) for m in masks] + [-first.astype(np.float32), -first.T.astype(np.float32)]
    return np.stack(out + [level(2 ** l).T.astype(np.float32) for l in range(1, LEVELS)])


def recurrence_phase(nc, name, ident, masks_dram, ends, alpha_d, beta_d, kappa_d, rho_d, v_d, y_dram):
    NP = RC
    turns = NCH // 2
    with Phase(nc, name) as ph:
        NM = 4 + LEVELS - 1
        masks = ph.sb("masks", [P, NM, P])
        ident4 = ph.sb("ident4", [P, NP, P])
        ins = [[ph.sb(f"in{g}{s}", [P, 5, NP, P]) for s in range(2)] for g in range(2)]
        tile = lambda n: [ph.sb(f"{n}{s}", [P, NP, P]) for s in range(2)]
        at_sb, bt_sb, rb_sb, rk_sb, lt_sb, t_sb, x_sb, xt_sb = (tile(n) for n in ("at", "bt", "rb", "rk", "lt", "t", "x", "xt"))
        beta_tok, kappa_tok, v_tok, w_sb, u_sb = (tile(n) for n in ("beta_tok", "kappa_tok", "v_tok", "w", "u"))
        y_sb = [ph.sb(f"y{s}", [P, NP, CHUNK]) for s in range(2)]
        state, grown = ph.sb("state", [P, NP, P]), ph.sb("grown", [P, NP, P])
        bank = [[ph.ps(f"bank{s}{b}", [P, NP, P]) for b in range(4)] for s in range(2)]
        zeroed, masks_loaded, ready4 = ph.sem("zeroed"), ph.sem("masks_loaded"), ph.sem("ready4")
        loaded = [[ph.sem(f"loaded{g}{s}") for s in range(2)] for g in range(2)]
        turn_done, scores_ready, evacuated = ph.sem("turn_done"), ph.sem("scores_ready"), ph.sem("evacuated")
        tok_ready, tok_copied, rk_masked, own = ph.sem("tok_ready"), ph.sem("tok_copied"), ph.sem("rk_masked"), ph.sem("own")
        level_ready, t_ready, t_copied = ph.sem("level_ready"), ph.sem("t_ready"), ph.sem("t_copied")
        xw_ready, x_ready = ph.sem("xw_ready"), ph.sem("x_ready")
        rhs_ready, rhs_copied, u_ready, u_copied = ph.sem("rhs_ready"), ph.sem("rhs_copied"), ph.sem("u_ready"), ph.sem("u_copied")
        y_ready, y_copied, grown_ready, grown_sum, state_ready = (ph.sem("y_ready"), ph.sem("y_copied"), ph.sem("grown_ready"),
                                                                  ph.sem("grown_sum"), ph.sem("state_ready"))
        stored = [ph.sem(f"stored{s}") for s in range(2)]
        block = ph.block()
        NLV = LEVELS - 1
        X_PER = 2 * (2 + 2 * (NLV - 1) + 1)
        OWN = 2 * 3

        def x_at(l, s):
            if l < 0:
                return 2 * s + 2
            return 4 + 4 * l + 2 * s + 2 if l < NLV - 1 else 4 + 4 * l + s + 1

        def spread(mask):
            return masks[:, mask:mask + 1, :].to_broadcast([P, NP, P])

        @block.sync
        def _(sp):
            sp.dma_start(masks[:, :, :], masks_dram.rearrange("m p n -> p m n")).then_inc(masks_loaded, 16)
            sp.wait_ge(zeroed, 4)
            with sp.Fori(0, turns // 2) as it:
                for g in range(2):
                    sp.wait_ge(turn_done, it * 2 + (g + 1))
                    for s in range(2):
                        t0 = ((it * 2 + g) * 2 + s) * CHUNK
                        for n, src in enumerate((alpha_d, beta_d, kappa_d, rho_d, v_d)):
                            rows = src.rearrange("(c p) t -> p c t", p=P)
                            for h in range(2):
                                sp.dma_start(ins[g][s][64 * h:64 * h + 64, n, :, 64 * h:64 * h + 64],
                                             rows[64 * h:64 * h + 64, :, ds(t0, CHUNK)]).then_inc(loaded[g][s], 16)

        @block.gpsimd
        def _(pool):
            for g in range(2):
                for s in range(2):
                    nc.gpsimd.memset(ins[g][s][:, :, :, :], 0.0).then_inc(zeroed, 1)
            pool.wait_ge(masks_loaded, 16)
            pool.wait_ge(zeroed, 4)
            with pool.Fori(0, turns) as turn:
                for l in range(NLV):
                    for s in range(2):
                        if l == 0:
                            pool.wait_ge(evacuated, turn * 8 + (4 * s + 1))
                        else:
                            pool.wait_ge(t_ready, turn * (2 * NLV) + (2 * (l - 1) + s + 1))
                        nc.gpsimd.tensor_tensor(lt_sb[s][:, :, :], at_sb[s][:, :, :], spread(4 + l), ALU.mult).then_inc(level_ready, 1)

        @block.tensor
        def _(pe):
            for g in range(2):
                pe.sem_inc(turn_done, 1)
            with pe.Fori(0, turns // 2) as it:
                for g in range(2):
                    turn = it * 2 + g

                    def product(out, lhsT, rhs, start=True, stop=True):
                        for q in range(NP):
                            mm = nc.tensor.matmul(out[:, q, :], lhsT[:, q, :], rhs[:, q, :], start=start, stop=stop,
                                                  skip_group_check=True)
                        return mm

                    def products(out, pairs):
                        for q in range(NP):
                            for n, (lhsT, rhs) in enumerate(pairs):
                                mm = nc.tensor.matmul(out[:, q, :], lhsT[:, q, :], rhs[:, q, :], start=(n == 0),
                                                      stop=(n == len(pairs) - 1), skip_group_check=True)
                        return mm

                    parts = [[ins[g][s][:, n] for n in range(5)] for s in range(2)]
                    for s in range(2):
                        al, be, ka, rh, _ = parts[s]
                        pe.wait_ge(loaded[g][s], it * 160 + 160)
                        for b, (lhsT, rhs) in enumerate(((be, al), (al, be), (ka, al), (be, rh))):
                            product(bank[s][b], lhsT, rhs).then_inc(scores_ready, 1)
                    for s in range(2):
                        al, be, ka, rh, v = parts[s]
                        pe.wait_ge(evacuated, turn * 8 + (4 * s + 1))
                        product(bank[s][0], ka, rh).then_inc(tok_ready, 1)
                        for b, src in ((1, be), (2, ka), (3, v)):
                            pe.wait_ge(evacuated, turn * 8 + (4 * s + b + 1))
                            for q in range(NP):
                                tr = nc.tensor.transpose(bank[s][b][:, q, :], src[:, q, :], ident[:, :])
                            tr.then_inc(tok_ready, 1)
                    for l in range(NLV):
                        for s in range(2):
                            pe.wait_ge(level_ready, turn * (2 * NLV) + (2 * l + s + 1))
                            pe.wait_ge(x_ready, turn * X_PER + x_at(l - 1, s))
                            if l == 0:
                                pe.wait_ge(rk_masked, turn * 2 + (s + 1))
                            product(bank[s][0], lt_sb[s], x_sb[s]).then_inc(t_ready, 1)
                        for s in range(2):
                            pe.wait_ge(t_copied, turn * (2 * NLV) + (2 * l + s + 1))
                            if l == 0:
                                pe.wait_ge(tok_copied, turn * 6 + (3 * s + 3))
                            if l < NLV - 1:
                                product(bank[s][1], xt_sb[s], t_sb[s])
                            product(bank[s][2], t_sb[s], xt_sb[s]).then_inc(xw_ready, 1)
                    for s in range(2):
                        al, be, ka, rh, _ = parts[s]
                        pe.wait_ge(x_ready, turn * X_PER + x_at(NLV - 1, s))
                        pe.wait_ge(state_ready, turn * 2 + (s + 1))
                        products(bank[s][0], ((bt_sb[s], v_tok[s]), (al, state))).then_inc(rhs_ready, 1)
                        pe.wait_ge(rhs_copied, turn * 2 + (s + 1))
                        product(bank[s][1], xt_sb[s], w_sb[s]).then_inc(u_ready, 1)
                        pe.wait_ge(u_copied, turn * 2 + (s + 1))
                        products(bank[s][3], ((kappa_tok[s], v_tok[s]), (beta_tok[s], u_sb[s]))).then_inc(grown_ready, 1)
                        products(bank[s][2], ((state, rh), (v_tok[s], rk_sb[s]), (u_sb[s], rb_sb[s]))).then_inc(y_ready, 1)
                    pe.wait_ge(y_copied, turn * 4 + 4)
                    pe.wait_ge(state_ready, turn * 2 + 3)
                    pe.sem_inc(turn_done, 1)

        @block.vector
        def _(dve):
            tt = nc.vector.tensor_tensor
            nc.vector.memset(state[:, :, :], 0.0).then_inc(state_ready, 1)
            for q in range(NP):
                nc.vector.tensor_copy(ident4[:, q, :], ident[:, :]).then_inc(ready4, 1)
            dve.wait_ge(ready4, NP)
            dve.wait_ge(masks_loaded, 16)
            with dve.Fori(0, turns) as turn:
                for s in range(2):
                    def scores(b):
                        dve.wait_ge(scores_ready, turn * 8 + (4 * s + b + 1))
                        return bank[s][b][:, :, :]

                    tt(at_sb[s][:, :, :], scores(0), spread(0), ALU.mult).then_inc(evacuated, 1)
                    tt(x_sb[s][:, :, :], scores(1), spread(2), ALU.mult).then_inc(evacuated, 1)
                    tt(bt_sb[s][:, :, :], scores(2), spread(0), ALU.mult).then_inc(evacuated, 1)
                    tt(rb_sb[s][:, :, :], scores(3), spread(1), ALU.mult).then_inc(evacuated, 1)
                    dve.wait_ge(evacuated, turn * 8 + (4 * s + 4))
                    tt(xt_sb[s][:, :, :], at_sb[s][:, :, :], spread(3), ALU.mult).then_inc(own, 1)
                    tt(x_sb[s][:, :, :], x_sb[s][:, :, :], ident4[:, :, :], ALU.add).then_inc(x_ready, 1)
                    dve.wait_ge(own, turn * 2 + (s + 1))
                    tt(xt_sb[s][:, :, :], xt_sb[s][:, :, :], ident4[:, :, :], ALU.add).then_inc(x_ready, 1)
                for s in range(2):
                    dve.wait_ge(tok_ready, turn * 8 + (4 * s + 1))
                    tt(rk_sb[s][:, :, :], bank[s][0][:, :, :], spread(1), ALU.mult).then_inc(rk_masked, 1)
                for l in range(NLV):
                    for s in range(2):
                        dve.wait_ge(xw_ready, turn * (2 * NLV) + (2 * l + s + 1))
                        dve.wait_ge(x_ready, turn * X_PER + x_at(l - 1, s))
                        if l < NLV - 1:
                            tt(x_sb[s][:, :, :], x_sb[s][:, :, :], bank[s][1][:, :, :], ALU.subtract).then_inc(x_ready, 1)
                        tt(xt_sb[s][:, :, :], xt_sb[s][:, :, :], bank[s][2][:, :, :], ALU.subtract).then_inc(x_ready, 1)
                for s in range(2):
                    dve.wait_ge(u_ready, turn * 2 + (s + 1))
                    nc.vector.tensor_copy(u_sb[s][:, :, :], bank[s][1][:, :, :]).then_inc(u_copied, 1)
                    dve.wait_ge(grown_ready, turn * 2 + (s + 1))
                    tt(grown[:, :, :], bank[s][3][:, :, :], state[:, :, :], ALU.add).then_inc(grown_sum, 1)
                    dve.wait_ge(grown_sum, turn * 2 + (s + 1))
                    dve.wait_ge(y_ready, turn * 2 + (s + 1))
                    tt(state[:, :, :], grown[:, :, :], ends[:, :, ds(turn * 2 + s, 1)].to_broadcast([P, NP, P]),
                       ALU.mult).then_inc(state_ready, 1)

        @block.scalar
        def _(act):
            for s in range(2):
                act.sem_inc(stored[s], 16)
            with act.Fori(0, turns) as turn:
                for s in range(2):
                    for n, dst in enumerate((beta_tok, kappa_tok, v_tok)):
                        act.wait_ge(tok_ready, turn * 8 + (4 * s + n + 2))
                        nc.scalar.activation(dst[s][:, :, :], bank[s][n + 1][:, :, :], ACT.Copy).then_inc(tok_copied, 1)
                for l in range(NLV):
                    for s in range(2):
                        act.wait_ge(t_ready, turn * (2 * NLV) + (2 * l + s + 1))
                        nc.scalar.activation(t_sb[s][:, :, :], bank[s][0][:, :, :], ACT.Copy).then_inc(t_copied, 1)
                for s in range(2):
                    act.wait_ge(rhs_ready, turn * 2 + (s + 1))
                    nc.scalar.activation(w_sb[s][:, :, :], bank[s][0][:, :, :], ACT.Copy, scale=-1.0).then_inc(rhs_copied, 1)
                    act.wait_ge(y_ready, turn * 2 + (s + 1))
                    act.wait_ge(stored[s], turn * 16 + 16)
                    for h in range(2):
                        r = slice(64 * h, 64 * h + 64)
                        nc.scalar.activation(y_sb[s][r, :, :], bank[s][2][r, :, r], ACT.Copy).then_inc(y_copied, 1)
                    act.wait_ge(y_copied, turn * 4 + (2 * s + 2))
                    act.dma_start(y_dram.rearrange("(c p) t -> p c t", p=P)[:, :, ds((turn * 2 + s) * CHUNK, CHUNK)],
                                  y_sb[s][:, :, :]).then_inc(stored[s], 16)
            for s in range(2):
                act.wait_ge(stored[s], 16 * turns + 16)


def center_phase(nc, name, block_ones, rows, dst):
    C = len(rows)
    steps = [(c, h) for c in range(C) for h in range(2)]
    with Phase(nc, name) as ph:
        sums = [ph.ps(f"sums{b}", [P, HALF]) for b in range(2)]
        loaded, sums_ready, ready = ph.sem("loaded"), ph.sem("sums_ready"), ph.sem("ready")
        block = ph.block()

        @block.sync
        def _(sp):
            for c in range(C):
                sp.dma_start(dst[:, c, :], rows[c]).then_inc(loaded, 16)

        @block.tensor
        def _(pe):
            pe.wait_ge(loaded, 16 * C)
            for j, (c, h) in enumerate(steps):
                if j >= 2:
                    pe.wait_ge(ready, j - 1)
                nc.tensor.matmul(sums[j % 2][:, :], block_ones[:, :], dst[:, c, h * HALF:(h + 1) * HALF], start=True,
                                 stop=True).then_inc(sums_ready, 1)

        @block.vector
        def _(dve):
            dve.wait_ge(loaded, 16 * C)
            for j, (c, h) in enumerate(steps):
                part = dst[:, c, h * HALF:(h + 1) * HALF]
                dve.wait_ge(sums_ready, j + 1)
                nc.vector.scalar_tensor_tensor(out=part, in0=sums[j % 2][:, :], scalar=-1.0 / 64, in1=part, op0=ALU.mult,
                                               op1=ALU.add).then_inc(ready, 1)


def add_phase(nc, name, dst, other):
    with Phase(nc, name) as ph:
        done = ph.sem("done")
        block = ph.block()

        @block.vector
        def _(dve):
            for c in range(dst.shape[1]):
                nc.vector.tensor_tensor(dst[:, c, :], dst[:, c, :], other[:, c, :], ALU.add).then_inc(done, 1)


def output_phase(nc, name, ident, x, out_dram):
    groups = 2 * (T // P)
    with Phase(nc, name) as ph:
        turned = [ph.ps(f"turned{b}", [P, 4, P]) for b in range(4)]
        rows = [ph.sb(f"rows{b}", [P, D]) for b in range(2)]
        turned_ready, copied, stored = ph.sem("turned_ready"), ph.sem("copied"), [ph.sem(f"stored{b}") for b in range(2)]
        block = ph.block()

        @block.tensor
        def _(pe):
            for g in range(groups):
                t, f0 = g // 2, 4 * (g % 2)
                if g >= 4:
                    pe.wait_ge(copied, g - 3)
                for b in range(4):
                    tr = nc.tensor.transpose(turned[g % 4][:, b, :], x[:, f0 + b, t * P:(t + 1) * P], ident[:, :])
                tr.then_inc(turned_ready, 1)

        @block.vector
        def _(dve):
            for g in range(groups):
                t, f0 = g // 2, 4 * (g % 2)
                if t >= 2:
                    dve.wait_ge(stored[t % 2], 16 * (t // 2))
                dve.wait_ge(turned_ready, g + 1)
                nc.vector.tensor_copy(rows[t % 2][:, f0 * P:(f0 + 4) * P].rearrange("p (b n) -> p b n", b=4),
                                      turned[g % 4][:, :, :]).then_inc(copied, 1)

        @block.sync
        def _(sp):
            for t in range(T // P):
                sp.wait_ge(copied, 2 * t + 2)
                sp.dma_start(out_dram[t * P:(t + 1) * P, :], rows[t % 2][:, :]).then_inc(stored[t % 2], 16)
            for b in range(2):
                sp.wait_ge(stored[b], 16 * (T // P // 2))


SB_W, CONV_W, MEM_W = 512, 256, 256
Q1, K1, V1 = 0, SB_W, 2 * SB_W
U1 = 3 * SB_W
B1, C1 = U1 + CONV_W, U1 + 2 * CONV_W
QM1 = U1 + 3 * CONV_W
GATE1 = QM1 + MEM_W
W1 = GATE1 + D
N_MEM = 256
Q2, K2, V2 = 0, 512, 640
HY2 = 768
FN2 = HY2 + 3 * 256
GATE2 = FN2 + 256
W2 = GATE2 + 3 * D
N_CTX = 256
CKV3 = 256
KR3 = CKV3 + 128
RW3 = KR3 + 64
Z3 = RW3 + 3 * 512 + 128
W3 = Z3 + D
MLA_HEADS, NOPE, ROPE = 4, 128, 64


def rows_of(a, row0=0, n=None):
    n = (a.shape[0] - row0) // P if n is None else n
    return [a[row0 + c * P:row0 + (c + 1) * P, :] for c in range(n)]


def pieces(vec):
    return [vec[c * P:(c + 1) * P] for c in range(vec.shape[0] // P)]


def first_block(nc, A, C, xT):
    ident, ones = C["ident"], C["ones"]
    scratch = lambda n, rows, cols=T: nc.dram_tensor(n, [rows, cols], F32).ap()
    p, y = scratch("proj1", W1), scratch("mixed1", D)
    mem_kv = scratch("mem_kv", 2 * MEM_W, N_MEM)
    with Phase(nc, "b1") as b1:
        hT = b1.sb("hT", [P, KD, T])
        all_chunks = [(list(range(KD)), D)]
        transpose_phase(nc, "b1_turn", ident, A["x"][0], xT, T)
        norm_phase(nc, "b1_norm", ones, xT, hT, all_chunks, pieces(A["g_in"][0]))
        gemm_phase(nc, "b1_in", hT, A["w_in"][0], D, 0, W1, out_dram=p)
        with Phase(nc, "b1m") as m:
            memT = m.sb("memT", [P, KD, N_MEM])
            transpose_phase(nc, "mem_turn", ident, A["mem"][0], memT, N_MEM)
            norm_phase(nc, "mem_norm", ones, memT, memT, all_chunks, pieces(A["g_mem"][0]), tokens=N_MEM)
            gemm_phase(nc, "mem_kv", memT, A["w_mem_kv"][0], D, 0, 2 * MEM_W, tokens=N_MEM, out_dram=mem_kv)
        stick_phase(nc, "stick", ident, C["strict"], C["neg_future"], C["neg_upper"], C["neg_ones"],
                    p[Q1:Q1 + SB_W, :], p[K1:K1 + SB_W, :], p[V1:V1 + SB_W, :], y[0:SB_W, :], SB_W // 64)
        at = lambda row0: (lambda c: p[ds(c * P + row0, P), :])
        short_conv_phase(nc, "conv", 1, at(U1), at(C1), at(B1), A["conv_w"][0], A["conv_b"][0], 2,
                         lambda c: y[ds(c * P + SB_W, P), :])
        head = lambda a, row0: (lambda q, s: a[ds((q * 2 + s) * 64 + row0, 64), :])
        attend_phase(nc, "mem", ident, MEM_W // 64, [(64, head(p, QM1), head(mem_kv, 0))], head(mem_kv, MEM_W),
                     y, SB_W + CONV_W, 64, N_MEM, 64 ** -0.5)
        norm_phase(nc, "b1_out_norm", ones, hT, hT, [([0, 1, 2, 3], SB_W), ([4, 5], CONV_W), ([6, 7], MEM_W)],
                   pieces(A["g_sb_out"][0]) + pieces(A["g_conv_out"][0]) + pieces(A["g_mem_out"][0]), src_dram=rows_of(y))
        gate_phase(nc, "b1_gate", hT, at(GATE1))
        gemm_phase(nc, "b1_out", hT, A["w_out"][0], D, 0, D, residual=xT)
        norm_phase(nc, "b1_final", ones, xT, xT, all_chunks, pieces(A["g_final"]))


def second_block(nc, A, C, xT):
    ident, ones, block_ones = C["ident"], C["ones"], C["block_ones"]
    scratch = lambda n, rows, cols=T: nc.dram_tensor(n, [rows, cols], F32).ap()
    p, pc = scratch("proj2", W2), scratch("proj2_ctx", 256, N_CTX)
    q, kx, vx = scratch("q2", 512), scratch("k2", P, T + N_CTX), scratch("v2", P, T + N_CTX)
    att, hy, fn = scratch("att2", 512), scratch("hy2", 256), scratch("fn2", 256)
    w_in = A["w_in_2"][0]
    all_chunks = [(list(range(KD)), D)]
    with Phase(nc, "b2") as b2:
        cols = b2.sb("cols", [P, 6 * KD, 2])
        mod_phase(nc, "mod", ident, [A["c_2"][0], A["c_ctx_2"]], A["w_mod_2"][0], A["b_mod_2"], cols)
        shift1, scale1, gain1, shift2, scale2, gain2 = (cols[:, KD * j:KD * (j + 1), 0] for j in range(6))
        ctx_shift, ctx_scale = (cols[:, KD * j:KD * (j + 1), 1] for j in range(2))
        norm1 = pieces(A["norm1_g_2"][0])
        with Phase(nc, "b2c") as c:
            ctxT, k_sb = c.sb("ctxT", [P, KD, N_CTX]), c.sb("k", [P, 1, N_CTX])
            transpose_phase(nc, "ctx_turn", ident, A["ctx_2"][0], ctxT, N_CTX)
            norm_phase(nc, "ctx_norm", ones, ctxT, ctxT, all_chunks, norm1, tokens=N_CTX, scale_cols=ctx_scale,
                       shift_cols=ctx_shift)
            gemm_phase(nc, "ctx_kv", ctxT, w_in, D, K2, 256, tokens=N_CTX, out_dram=pc)
            norm_phase(nc, "ctx_k_norm", block_ones, k_sb, k_sb, [([0], 64)], [A["k_gain_2"][0]], tokens=N_CTX,
                       src_dram=[pc[0:P, :]], store_dram=[kx[:, T:T + N_CTX]])
        with Phase(nc, "b2m") as m:
            hT = m.sb("hT", [P, KD, T])
            norm_phase(nc, "b2_norm", ones, xT, hT, all_chunks, norm1, scale_cols=scale1, shift_cols=shift1)
            gemm_phase(nc, "b2_in", hT, w_in, D, 0, W2, out_dram=p)
        with Phase(nc, "b2q") as m:
            qk, rope_cos, rope_sin = m.sb("qk", [P, 5, T]), m.sb("cos", [P, T]), m.sb("sin", [P, T])
            load_phase(nc, "b2_tables", [(rope_cos[:, :], A["grid_cos"]), (rope_sin[:, :], A["grid_sin"]),
                                         (vx[:, 0:T], p[V2:V2 + P, :]), (vx[:, T:T + N_CTX], pc[P:2 * P, :])])
            norm_phase(nc, "qk_norm", block_ones, qk, qk, [([n], 64) for n in range(5)],
                       [A["q_gain_2"][0]] * 4 + [A["k_gain_2"][0]], src_dram=rows_of(p, Q2, 5))
            rope_phase(nc, "qk_rope", C["pair_rot"], qk, range(5), rope_cos, rope_sin,
                       rows_of(q) + [kx[:, 0:T]])
        attend_phase(nc, "gqa", ident, 8, [(64, lambda r, s: q[ds((r * 2 + s) * 64, 64), :],
                                            lambda r, s: kx[ds((r // 2) * 64, 64), :])],
                     lambda r, s: vx[ds((r // 2) * 64, 64), :], att, 0, 64, T + N_CTX, 64 ** -0.5)
        hyena(nc, A, C, p, hy)
        over_channels = scratch("over_channels", 2 * T, 256)
        for n, table in enumerate(("channel_cos", "channel_sin")):
            gemm_phase(nc, f"{table}_dft", None, p[FN2:FN2 + 256, :], 256, 0, T, tokens=256, act_dram=A[table],
                       out_dram=over_channels, out_row0=T * n)
        stream_gemm_phase(nc, "token_dft", over_channels, A["token_tables"], fn)
        with Phase(nc, "b2o") as m:
            merged = m.sb("merged", [P, KD, T])
            merge_phase(nc, "merge", [att, hy, fn], A["w_branch_2"][0],
                        lambda b, n: p[ds(n * P + (GATE2 + b * D), P), :], merged)
            gemm_phase(nc, "b2_out", merged, A["w_out_2"][0], D, 0, D, residual=xT, res_gain=gain1)
        with Phase(nc, "b2e") as m:
            h_rows, expert_sums = scratch("h_rows", T, D), scratch("expert_sums", T, D)
            token_of_slot, weight_of_slot = m.sb("token_of_slot", [P, N_EXPERTS], U32), m.sb("weight_of_slot", [P, N_EXPERTS])
            with Phase(nc, "b2r") as r:
                hT = r.sb("hT", [P, KD, T])
                norm_phase(nc, "b2_norm2", ones, xT, hT, all_chunks, pieces(A["norm2_g_2"][0]), scale_cols=scale2,
                           shift_cols=shift2)
                route_phase(nc, "route", ident, C["iota_row"], C["iota_col"], hT, A["w_router_2"][0], h_rows,
                            token_of_slot, weight_of_slot)
            expert_phase(nc, "experts", ident, h_rows, token_of_slot, weight_of_slot,
                         A["w_gate_2"][0], A["w_up_2"][0], A["w_down_2"][0], expert_sums)
            add_turned_phase(nc, "add_experts", ident, expert_sums, gain2, xT)
        norm_phase(nc, "b2_final", ones, xT, xT, all_chunks, pieces(A["final_g_2"]))


def hyena(nc, A, C, p, hy):
    ident, ones, W = C["ident"], C["ones"], 256
    scratch = lambda n, rows, cols=T: nc.dram_tensor(n, [rows, cols], F32).ap()
    short, spec = scratch("hy_short", 3 * W), scratch("hy_spectrum", 2 * T, 2 * W)
    z_spec, y_spec = scratch("hy_z_spectrum", 2 * T, W), scratch("hy_y_spectrum", 2 * T, W)
    y, z1 = scratch("hy_y", W), scratch("hy_z1", W)
    short_conv_phase(nc, "hy_short", 3, lambda c: p[ds(c * P + HY2, P), :], None, None, A["hy_short_w_2"][0],
                     A["hy_short_b_2"][0], 1, lambda c: short[ds(c * P, P), :])
    with Phase(nc, "hy") as m:
        inv_norm = m.sb("inv_norm", [P, 2 * W])
        with Phase(nc, "hyf") as f:
            even, odd = f.sb("even", [P, T // P, 2 * W]), f.sb("odd", [P, T // P, 2 * W])
            filter_phase(nc, "filter", ones, A["filter_features"], A["hy_f_w1_2"][0], A["hy_f_b1_2"][0],
                         A["hy_f_w2_2"][0], A["hy_f_b2_2"][0], A["hy_f_w3_2"][0], A["hy_f_freq_2"][0],
                         A["decay"], A["decay_back"], even, odd, inv_norm)
            gemm_phase(nc, "spec_cos", even, A["dft"], T, 0, T, tokens=2 * W, out_dram=spec, out_row0=0)
            gemm_phase(nc, "spec_sin", odd, A["dft"], T, T, T, tokens=2 * W, out_dram=spec, out_row0=T)
        zT = m.sb("zT", [P, T // P, W])
        for o in range(2):
            z = short[0:W, :] if o == 0 else z1
            transpose_phase(nc, f"z_turn{o}", ident, z, zT, W)
            gemm_phase(nc, f"z_dft{o}", zT, A["dft"], T, 0, 2 * T, tokens=W, out_dram=z_spec)
            spectrum_phase(nc, f"times_spec{o}", z_spec, spec, o * W, inv_norm, y_spec)
            stream_gemm_phase(nc, f"inv_dft{o}", y_spec, A["inverse_dft"], y)
            skip_gate_phase(nc, f"skip_gate{o}", y, z, short[W * (o + 1):W * (o + 2), :], A["hy_bias_2"][0][o],
                            z1 if o == 0 else hy)


def third_block(nc, A, C, xT):
    ident, ones, block_ones = C["ident"], C["ones"], C["block_ones"]
    scratch = lambda n, rows, cols=T: nc.dram_tensor(n, [rows, cols], F32).ap()
    p, y = scratch("proj3", W3), scratch("mixed3", D)
    all_chunks = [(list(range(KD)), D)]
    with Phase(nc, "b3a") as m:
        hT = m.sb("hT", [P, KD, T])
        norm_phase(nc, "b3_norm", ones, xT, hT, all_chunks, pieces(A["norm_pre_g_3"][0]))
        gemm_phase(nc, "b3_in", hT, A["w_in_3"][0], D, 0, W3, out_dram=p)
    latent_attention(nc, A, C, p, y[0:512, :])
    with Phase(nc, "b3c") as m:
        ends, bonus = m.sb("ends", [P, 4, T // 64]), m.sb("bonus", [P, 4, T])
        ps = scratch("shifted3", 3 * 512 + P)
        alpha, beta, kappa, rho, wkv = (scratch(f"rw_{n}", 512) for n in ("alpha", "beta", "kappa", "rho", "wkv"))
        token_shift_phase(nc, "shift", 13, lambda c: p[ds(c * P + RW3, P), :], A["rw_mu_3"][0],
                          lambda c: ps[ds(c * P, P), :])
        with Phase(nc, "b3i") as i:
            decay, rate, kk = (i.sb(n, [P, 4, T]) for n in ("decay", "rate", "kk"))
            lora_phase(nc, "lora", ps[1536:1664, :], A["rw_w2_3"][0], A["rw_a2_3"][0], A["rw_w0_3"][0],
                       A["rw_a0_3"][0], decay, rate)
            scale_rows_phase(nc, "kk_scale", rows_of(ps, 512, 4), A["rw_k_k_3"][0], kk)
            norm_phase(nc, "kk_norm", block_ones, kk, kk, [([c], 1) for c in range(4)], None, eps=1e-24, bound=ALU.max)
            recurrence_inputs_phase(nc, "rw_in", block_ones, lambda n: ps[n * P:(n + 1) * P, :], kk, decay, rate,
                                    A["rw_k_a_3"][0], A["rw_r_k_3"][0].rearrange("h n -> (h n)"), ends, bonus,
                                    [alpha, beta, kappa, rho])
        recurrence_phase(nc, "wkv", ident, A["recurrence_masks"], ends, alpha, beta, kappa, rho, ps[1024:1536, :], wkv)
        yT, ln_bias = m.sb("yT", [P, 4, T]), m.sb("ln_bias", [P, 4])
        with Phase(nc, "ln_b") as l:
            loaded = l.sem("loaded")
            block = l.block()

            @block.sync
            def _(sp):
                load_columns(sp, ln_bias[:, :], A["rw_ln_b_3"][0], loaded)
                sp.wait_ge(loaded, 16)
        center_phase(nc, "group_center", block_ones, rows_of(wkv), yT)
        norm_phase(nc, "group_norm", block_ones, yT, yT, [([c], 64) for c in range(4)], pieces(A["rw_ln_g_3"][0]),
                   eps=64e-5, shift_cols=ln_bias)
        add_phase(nc, "add_bonus", yT, bonus)
        load_phase(nc, "rw_store", [(y[512 + c * P:512 + (c + 1) * P, :], yT[:, c, :]) for c in range(4)])
    with Phase(nc, "b3o") as m:
        hT, out = m.sb("hT", [P, KD, T]), scratch("projected3", D)
        load_phase(nc, "b3_mixed", [(hT[:, c, :], r) for c, r in enumerate(rows_of(y))])
        gate_phase(nc, "b3_gate", hT, lambda c: p[ds(c * P + Z3, P), :])
        gemm_phase(nc, "b3_out", hT, A["w_out_3"][0], D, 0, D, out_dram=out)
        norm_phase(nc, "b3_post", ones, hT, hT, all_chunks, pieces(A["norm_post_g_3"][0]), src_dram=rows_of(out))
        add_phase(nc, "b3_residual", xT, hT)


def latent_attention(nc, A, C, p, y):
    ident, ones = C["ident"], C["ones"]
    scratch = lambda n, rows, cols=T: nc.dram_tensor(n, [rows, cols], F32).ap()
    uq, ukv = scratch("unfolded_q", MLA_HEADS * (NOPE + ROPE)), scratch("unfolded_kv", MLA_HEADS * 2 * NOPE)
    qr, kr = scratch("rotated_q", MLA_HEADS * ROPE), scratch("rotated_k", ROPE)
    with Phase(nc, "b3l") as m:
        latent = m.sb("latent", [P, 3, T])
        norm_phase(nc, "latent_norm", ones, latent, latent, [([0, 1], 256), ([2], 128)],
                   pieces(A["mla_q_norm_g_3"][0]) + pieces(A["mla_kv_norm_g_3"][0]), src_dram=rows_of(p, 0, 3))
        gemm_phase(nc, "unfold_q", latent[:, 0:2, :], A["mla_w_uq_3"][0], 256, 0, uq.shape[0], out_dram=uq)
        gemm_phase(nc, "unfold_kv", latent[:, 2:3, :], A["mla_w_ukv_3"][0], P, 0, ukv.shape[0], out_dram=ukv)
    with Phase(nc, "b3r") as m:
        rope, cos, sin = m.sb("rope", [P, 3, T]), m.sb("cos", [P, T]), m.sb("sin", [P, T])
        angle_phase(nc, "angles", A["positions_3"], A["rope_freq"], cos, sin)
        unrotated = [uq[(h * 3 + 2) * 64:(h * 3 + 3) * 64, :] for h in range(MLA_HEADS)] + [p[KR3:KR3 + ROPE, :]] * 2
        load_phase(nc, "rope_rows", [(rope[64 * (n % 2):64 * (n % 2) + 64, n // 2, :], r) for n, r in enumerate(unrotated)])
        rope_phase(nc, "mla_rope", C["half_rot"], rope, range(3), cos, sin, rows_of(qr) + [kr])
    head = lambda a, step, rows, row0=0: (lambda r, s: a[ds((r * 2 + s) * step + row0, rows), :])
    attend_phase(nc, "mla", ident, MLA_HEADS,
                 [(NOPE, head(uq, NOPE + ROPE, NOPE), head(ukv, 2 * NOPE, NOPE)),
                  (ROPE, head(qr, ROPE, ROPE), lambda r, s: kr[:, :])],
                 head(ukv, 2 * NOPE, NOPE, NOPE), y, 0, NOPE, T, (NOPE + ROPE) ** -0.5, causal_mask=C["causal"])


SQUARE_CONSTANTS = ("ident", "ones", "neg_ones", "strict", "neg_future", "neg_upper", "causal", "block_ones",
                    "iota_row", "iota_col", "pair_rot", "half_rot")


def three_blocks(nc, A, out):
    with Phase(nc, "top") as top:
        squares = top.sb("squares", [P, len(SQUARE_CONSTANTS), P])
        xT = top.sb("xT", [P, KD, T])
        load_phase(nc, "constants", [(squares[:, :, :], A["squares"].rearrange("m p n -> p m n"))])
        C = {n: squares[:, j, :] for j, n in enumerate(SQUARE_CONSTANTS)}
        first_block(nc, A, C, xT)
        second_block(nc, A, C, xT)
        third_block(nc, A, C, xT)
        output_phase(nc, "output", C["ident"], xT, out[0])


def constants():
    f = np.float32
    i = np.arange(P)
    row, col = i[:, None], i[None, :]
    pair_rot, half_rot = np.zeros((P, P), f), np.zeros((P, P), f)
    for m in range(0, P, 2):
        pair_rot[m + 1, m], pair_rot[m, m + 1] = -1, 1
    for m in range(P):
        half_rot[(m + 32, m) if m % 64 < 32 else (m - 32, m)] = -1 if m % 64 < 32 else 1
    squares = dict(ident=row == col, ones=np.ones((P, P)), neg_ones=-np.ones((P, P)), strict=row < col,
                   neg_future=np.where(row < col, 0, -1e30), neg_upper=-(row >= col).astype(f),
                   causal=np.where(col <= row, 0, -1e30), block_ones=np.kron(np.eye(2), np.ones((64, 64))),
                   iota_row=np.broadcast_to(col, (P, P)), iota_col=np.broadcast_to(row, (P, P)),
                   pair_rot=pair_rot, half_rot=half_rot)
    out = {"squares": np.stack([squares[n].astype(f) for n in SQUARE_CONSTANTS])}
    inv = (f(10000.0) ** (-np.arange(0, 32, 2, dtype=f) / f(32))).astype(f)
    t = np.arange(T)
    ang = np.concatenate([(t // 64).astype(f)[:, None] * inv, (t % 64).astype(f)[:, None] * inv], axis=1)
    ang = np.tile(np.repeat(ang, 2, axis=1), (1, 2)).T
    out["grid_cos"], out["grid_sin"] = np.cos(ang).astype(f), np.sin(ang).astype(f)
    out["rope_freq"] = np.tile((f(10000.0) ** (-np.arange(0, 64, 2, dtype=f) / f(64))).astype(f), 4)[:, None]
    odd = np.pi * (2 * t[None, :] + 1) * t[:, None] / (2 * T)
    out["dft"] = np.concatenate([np.cos(odd), np.sin(odd)], axis=1).astype(f)
    out["inverse_dft"] = (np.concatenate([np.cos(odd).T, np.sin(odd).T], axis=0) / T).astype(f)
    pos = np.arange(T, dtype=f)
    tn = pos / f(T - 1)
    bands = np.linspace(1e-4, 15, 16, dtype=f)
    a = (f(2 * np.pi / T) * pos[:, None] * bands[None, :]).astype(f)
    out["filter_features"] = np.concatenate([tn[:, None], np.cos(a), -np.sin(a)], axis=1).astype(f).T
    deltas = np.abs(np.linspace(np.log(1e-2) / 1.5, np.log(1e-2) / 0.3, 256, dtype=f))
    out["decay"] = np.tile(np.exp(-tn[:, None] * deltas[None, :]).astype(f), (1, 2))
    out["decay_back"] = out["decay"].copy()
    out["decay_back"][0] = 0
    c = 2 * np.pi * np.outer(np.arange(64), np.arange(64)) / 64
    out["channel_cos"] = np.kron(np.eye(4), np.cos(c) / 256).astype(f)
    out["channel_sin"] = np.kron(np.eye(4), -np.sin(c) / 256).astype(f)
    ph = np.outer(t, t) % T * (2 * np.pi / T)
    out["token_tables"] = np.concatenate([np.cos(ph), np.sin(ph)], axis=0).astype(f)
    out["recurrence_masks"] = recurrence_masks()
    return out


def kernel(**inputs):
    import concourse.bacc as bacc
    from concourse.bass_utils import run_bass_kernel_spmd as run

    nc = bacc.Bacc("TRN2", target_bir_lowering=False, num_devices=1)
    arrays, A = {}, {}
    for name, a in list(inputs.items()) + list(constants().items()):
        a = np.ascontiguousarray(a)
        arrays[f"in_{name}"] = a
        A[name] = nc.dram_tensor(f"in_{name}", a.shape, mybir.dt.from_np(a.dtype), kind="ExternalInput").ap()
    out = nc.dram_tensor("out", (1, T, D), F32, kind="ExternalOutput").ap()
    three_blocks(nc, A, out)
    r = run(nc, [arrays], core_ids=[0])
    return r.results[0]["out"]
```
